# Optimizing a Trainium2 kernel written in Bass

```python
import jax, jax.numpy as jnp
from jax import lax
import numpy as np

D_MODEL = 2048
BATCH = 1
SEQ = 256
DEPTH = 1

MEM_LEN = 256
HEAD_DIM = 128
D_MIX = D_MODEL
N_MOBA_HEADS = D_MIX // 2 // HEAD_DIM
MOBA_WIDTH = N_MOBA_HEADS * HEAD_DIM
N_MEM_HEADS = 4
MEM_WIDTH = N_MEM_HEADS * HEAD_DIM
POOL_WIDTH = D_MIX - MOBA_WIDTH - MEM_WIDTH
POOL_WINDOWS = (2, 4, 8, 16)
N_POOL_GROUPS = len(POOL_WINDOWS)
POOL_GROUP_DIM = POOL_WIDTH // N_POOL_GROUPS
MOBA_BLOCK = 256
MOBA_TOPK = 3
QUERY_CHUNK = 32
EPS = 1e-6
IN_SIZES = (MOBA_WIDTH, MOBA_WIDTH, MOBA_WIDTH, MOBA_WIDTH,
            POOL_WIDTH, POOL_WIDTH,
            MEM_WIDTH, MEM_WIDTH)
D_IN = sum(IN_SIZES)
IN_OFFSETS = [int(o) for o in np.cumsum(IN_SIZES)[:-1]]

kernel_name = "hybrid_moba_pool_memory_layer"

def rmsnorm(x, g):
    xf = x.astype(jnp.float32)
    y = xf * lax.rsqrt(jnp.mean(xf * xf, axis=-1, keepdims=True) + EPS)
    return (y * g.astype(jnp.float32)).astype(x.dtype)

def moba_attention(q, k, v):
    B, S, H, Dh = q.shape
    nb = -(-S // MOBA_BLOCK)
    s_pad = nb * MOBA_BLOCK
    pad = ((0, 0), (0, 0), (0, s_pad - S), (0, 0))
    q = jnp.pad(q.transpose(0, 2, 1, 3), pad)
    k = jnp.pad(k.transpose(0, 2, 1, 3), pad)
    v = jnp.pad(v.transpose(0, 2, 1, 3), pad)
    k_blk = k.reshape(B, H, nb, MOBA_BLOCK, Dh)
    v_blk = v.reshape(B, H, nb, MOBA_BLOCK, Dh)
    k_mean = jnp.mean(k_blk.astype(jnp.float32), axis=3)
    n_chunks = s_pad // QUERY_CHUNK
    q_chunks = q.reshape(B, H, n_chunks, QUERY_CHUNK, Dh).transpose(2, 0, 1, 3, 4)
    topk = min(MOBA_TOPK, nb - 1)
    scale = Dh ** -0.5
    b_ix = jnp.arange(B)[:, None, None, None]
    h_ix = jnp.arange(H)[None, :, None, None]
    blk_ids = jnp.arange(nb)

    def chunk(args):
        qc, c = args
        start = c * QUERY_CHUNK
        blk = start // MOBA_BLOCK
        qpos = start + jnp.arange(QUERY_CHUNK)
        kpos = blk * MOBA_BLOCK + jnp.arange(MOBA_BLOCK)
        k_own = lax.dynamic_index_in_dim(k_blk, blk, axis=2, keepdims=False)
        v_own = lax.dynamic_index_in_dim(v_blk, blk, axis=2, keepdims=False)
        s_own = jnp.einsum('bhqd,bhkd->bhqk', qc, k_own).astype(jnp.float32) * scale
        s_own = jnp.where(kpos[None, :] <= qpos[:, None], s_own, -jnp.inf)
        if topk == 0:
            p = jax.nn.softmax(s_own, axis=-1).astype(v.dtype)
            return jnp.einsum('bhqk,bhkd->bhqd', p, v_own)
        gate = jnp.einsum('bhqd,bhnd->bhqn', qc.astype(jnp.float32), k_mean)
        gate = jnp.where(blk_ids < blk, gate, -jnp.inf)
        _, idx = lax.top_k(gate, topk)
        valid = idx < blk
        k_sel = k_blk[b_ix, h_ix, idx]
        v_sel = v_blk[b_ix, h_ix, idx]
        s_sel = jnp.einsum('bhqd,bhqnkd->bhqnk', qc, k_sel).astype(jnp.float32) * scale
        s_sel = jnp.where(valid[..., None], s_sel, -jnp.inf)
        s_sel = s_sel.reshape(B, H, QUERY_CHUNK, topk * MOBA_BLOCK)
        p = jax.nn.softmax(jnp.concatenate([s_sel, s_own], axis=-1), axis=-1).astype(v.dtype)
        p_sel = p[..., :topk * MOBA_BLOCK].reshape(B, H, QUERY_CHUNK, topk, MOBA_BLOCK)
        p_own = p[..., topk * MOBA_BLOCK:]
        return (jnp.einsum('bhqnk,bhqnkd->bhqd', p_sel, v_sel)
                + jnp.einsum('bhqk,bhkd->bhqd', p_own, v_own))

    out = lax.map(chunk, (q_chunks, jnp.arange(n_chunks)))
    out = out.transpose(1, 0, 3, 2, 4).reshape(B, s_pad, H, Dh)
    return out[:, :S]

def multiscale_pool(u, w_pool, pool_scale):
    B, S, _ = u.shape
    uf = u.astype(jnp.float32)
    cs = jnp.cumsum(uf, axis=1)
    t = jnp.arange(S)
    outs = []
    for g, w in enumerate(POOL_WINDOWS):
        csg = cs[..., g * POOL_GROUP_DIM:(g + 1) * POOL_GROUP_DIM]
        prev = jnp.pad(csg, ((0, 0), (w, 0), (0, 0)))[:, :S]
        cnt = jnp.minimum(t + 1, w).astype(jnp.float32)[None, :, None]
        outs.append((csg - prev) / cnt)
    pooled = jnp.stack(outs, axis=2) - uf.reshape(B, S, N_POOL_GROUPS, POOL_GROUP_DIM)
    mixed = jnp.einsum('bsgc,gcd->bsgd', pooled.astype(u.dtype), w_pool)
    return mixed.reshape(B, S, POOL_WIDTH) * pool_scale

def memory_attention(q, mem_k, mem_v):
    s = jnp.einsum('bshd,bmhd->bhsm', q, mem_k).astype(jnp.float32) * (HEAD_DIM ** -0.5)
    p = jax.nn.softmax(s, axis=-1).astype(mem_v.dtype)
    return jnp.einsum('bhsm,bmhd->bshd', p, mem_v)

def hybrid_layer(x, mem, norm_g, mem_norm_g, w_in, w_mem_kv, w_pool, pool_scale, w_out):
    B, S, _ = x.shape
    h = rmsnorm(x, norm_g)
    z = h @ w_in
    q_a, k_a, v_a, g_a, u_p, g_p, q_m, g_m = jnp.split(z, IN_OFFSETS, axis=-1)
    hd = (B, S, N_MOBA_HEADS, HEAD_DIM)
    y_a = moba_attention(q_a.reshape(hd), k_a.reshape(hd), v_a.reshape(hd))
    y_a = y_a.reshape(B, S, MOBA_WIDTH) * jax.nn.silu(g_a)
    y_p = multiscale_pool(u_p, w_pool, pool_scale) * jax.nn.silu(g_p)
    mem_h = rmsnorm(mem, mem_norm_g)
    mk, mv = jnp.split(mem_h @ w_mem_kv, 2, axis=-1)
    M = mem.shape[1]
    y_m = memory_attention(q_m.reshape(B, S, N_MEM_HEADS, HEAD_DIM),
                           mk.reshape(B, M, N_MEM_HEADS, HEAD_DIM),
                           mv.reshape(B, M, N_MEM_HEADS, HEAD_DIM))
    y_m = y_m.reshape(B, S, MEM_WIDTH) * jax.nn.silu(g_m)
    y = jnp.concatenate([y_a, y_p, y_m], axis=-1) @ w_out
    return x + y

def setup_inputs(seed: int = 0) -> dict:
    key = jax.random.key(seed)
    ks = jax.random.split(key, 11)
    f32 = jnp.float32
    x = jax.random.normal(ks[0], (BATCH, SEQ, D_MODEL), f32)
    mem = jax.random.normal(ks[1], (BATCH, MEM_LEN, D_MODEL), f32)
    norm_g = 1.0 + 0.02 * jax.random.normal(ks[2], (DEPTH, D_MODEL), f32)
    mem_norm_g = 1.0 + 0.02 * jax.random.normal(ks[3], (DEPTH, D_MODEL), f32)
    w_in = jax.random.normal(ks[4], (DEPTH, D_MODEL, D_IN), f32) * D_MODEL ** -0.5
    w_mem_kv = jax.random.normal(ks[5], (DEPTH, D_MODEL, 2 * MEM_WIDTH), f32) * D_MODEL ** -0.5
    w_pool = jax.random.normal(ks[6], (DEPTH, N_POOL_GROUPS, POOL_GROUP_DIM, POOL_GROUP_DIM), f32) * POOL_GROUP_DIM ** -0.5
    pool_scale = 1.0 + 0.1 * jax.random.normal(ks[7], (DEPTH, POOL_WIDTH), f32)
    w_out = jax.random.normal(ks[8], (DEPTH, D_MIX, D_MODEL), f32) * D_MIX ** -0.5
    final_norm_g = 1.0 + 0.02 * jax.random.normal(ks[9], (D_MODEL,), f32)
    return {"x": x, "mem": mem, "norm_g": norm_g, "mem_norm_g": mem_norm_g,
            "w_in": w_in, "w_mem_kv": w_mem_kv, "w_pool": w_pool,
            "pool_scale": pool_scale, "w_out": w_out, "final_norm_g": final_norm_g}

def reference(x, mem, norm_g, mem_norm_g, w_in, w_mem_kv, w_pool, pool_scale, w_out, final_norm_g):
    for l in range(DEPTH):
        x = hybrid_layer(x, mem, norm_g[l], mem_norm_g[l], w_in[l], w_mem_kv[l],
                         w_pool[l], pool_scale[l], w_out[l])
    return rmsnorm(x, final_norm_g)


_drawn_inputs = setup_inputs


def setup_inputs(seed=0):
    import zlib

    import numpy as np

    out = dict(_drawn_inputs(seed))
    spreads = {}
    factors = {'norm_g': 7.001, 'mem_norm_g': 8.0, 'final_norm_g': 2.789}
    for name, (base, spread) in spreads.items():
        noise = np.random.default_rng([zlib.crc32(name.encode()), seed]).standard_normal(out[name].shape)
        drawn = base * np.exp(spread * noise) if base else spread * noise
        out[name] = __import__('jax').numpy.asarray(drawn.astype(out[name].dtype))
    for name, factor in factors.items():
        out[name] = (out[name] * factor).astype(out[name].dtype)
    return out
```

```python
from contextlib import ExitStack

import concourse.bass as bass
from concourse import mybir

F32 = mybir.dt.float32
F32R = mybir.dt.float32r
ALU = mybir.AluOpType
ACT = mybir.ActivationFunctionType
AX = mybir.AxisListType

P = 128
D = 2048
S = 256
M = 256
HD = 128
KT = D // P
COLS = 512
NF = COLS // P
TH = S // P
EPS = 1e-6
SCALE = HD ** -0.5
WINDOWS = (2, 4, 8, 16)
PAD = WINDOWS[-1] // 2
MASKED = -3.0e38

TPP = 2
PPG = KT // TPP
RAW = 8
SPLIT = 4

(MK, MV, Q0, Q1, K0, K1, V0, V1, GA0, GA1, U, GP, QM, GM, OUT0) = range(15)
GROUPS = OUT0 + D // COLS
LAST = GROUPS - 1
PIECES = GROUPS * PPG
TOKENS_ON_ROWS = (MV, V0, V1)
CAUSAL_JOBS = {V1: 0, GA0: 1}
MEM_JOB = GM
JOBS = (V1, GA0, GM)
BRANCHES = (V1, GA0, GP, GM)
GATES = (GA0, GA1, GP, GM)


def build(nc, x, mem, norm_g, mem_norm_g, w_in, w_mem_kv, w_pool, pool_scale, w_out, final_g, out):
    with ExitStack() as ctx:
        def sb(name, shape, dt=F32, stack=ctx):
            return stack.enter_context(nc.sbuf_tensor(name, shape, dt))

        def sem(name):
            return ctx.enter_context(nc.semaphore(name))

        w_raw = sb("w_raw", [P, RAW, TPP, COLS])
        w_hi = sb("w_hi", [P, SPLIT, TPP, COLS], F32R)
        w_lo = sb("w_lo", [P, SPLIT, TPP, COLS], F32R)
        early = ExitStack()
        xT = sb("xT", [P, KT, 2, S], F32R, early)
        early.close()
        w_end = sb("w_end", [P, PPG - SPLIT, 2, TPP, COLS], F32R)
        early = ExitStack()
        mem_nat = sb("mem_nat", [P, TH, D], F32, early)
        x_nat = sb("x_nat", [P, TH, D], F32, early)
        early.close()
        yT = sb("yT", [P, KT, 2, S], F32R)
        early = ExitStack()
        memT = sb("memT", [P, KT, 2, S], F32R, early)
        early.close()
        early = ExitStack()
        qT = sb("qT", [P, 2 * NF, S], F32, early)
        kT = sb("kT", [P, 2 * NF, S], F32, early)
        early.close()
        x_res = sb("x_res", [P, TH, D])
        early = ExitStack()
        qmT = sb("qmT", [P, NF, S], F32, early)
        early.close()
        v = sb("v", [P, TH, 2 * COLS])
        fg = sb("fg", [P, D])
        mkT = sb("mkT", [P, NF, S])
        mv = sb("mv", [P, TH, COLS])
        early = ExitStack()
        probs = sb("probs", [P, NF, 2 * S], F32, early)
        probsT = sb("probsT", [P, NF, 2 * S], F32, early)
        early.close()
        early = ExitStack()
        u_pad = sb("u_pad", [P, NF, PAD + S], F32, early)
        sum_a = sb("sum_a", [P, NF, PAD + S], F32, early)
        sum_b = sb("sum_b", [P, NF, PAD + S], F32, early)
        early.close()
        early = ExitStack()
        squares = sb("squares", [P, D], F32, early)
        end_scaled = sb("end_scaled", [P, TH, COLS], F32, early)
        early.close()
        probs_end = sb("probs_end", [P, 2 * NF, 2 * S])
        att = sb("att", [P, 2, NF, S])
        part_b = sb("part_b", [P, NF, S])
        gate = sb("gate", [P, NF, S])
        ident = sb("ident", [P, P])
        mask = sb("mask", [P, P])
        rows = sb("rows", [2 * KT + NF, P])
        cols = sb("cols", [P, 2 * KT + NF])
        wp = sb("wp", [P, NF, P])
        inv_cnt = sb("inv_cnt", [P, NF, WINDOWS[-1]])
        nmax = sb("nmax", [P, NF, 2])
        sums = sb("sums", [P, NF, 2])
        rsum = sb("rsum", [P, NF, 2])
        ssq_in = sb("ssq_in", [P, 2, TH])
        ms_in = sb("ms_in", [P, 2, TH])
        rstd_in = sb("rstd_in", [P, 2, TH])
        ssq = sb("ssq", [P, TH, D // COLS])
        sst = sb("sst", [P, TH])
        ms = sb("ms", [P, TH])
        rstd = sb("rstd", [P, TH])
        power = sb("power", [P, 2])

        ps = ctx.enter_context(nc.psum_tensor("ps", [P, 8, 512], F32))

        landed = [sem(f"landed{i}") for i in range(RAW)]
        rows_landed = sem("rows_landed")
        wp_landed = sem("wp_landed")
        mem_landed = [sem(f"mem_landed{i}") for i in range(TH)]
        x_landed = [sem(f"x_landed{i}") for i in range(TH)]
        fg_landed = sem("fg_landed")
        res_landed = sem("res_landed")
        hi_done = sem("hi_done")
        lo_done = sem("lo_done")
        piece_used = sem("piece_used")
        consts_ready = sem("consts_ready")
        pool_self = sem("pool_self")
        rows_turned = sem("rows_turned")
        cols_ready = sem("cols_ready")
        squared = sem("squared")
        ms_ready = sem("ms_ready")
        rstd_ready = sem("rstd_ready")
        scaled = sem("scaled")
        turned = sem("turned")
        turned_hi = sem("turned_hi")
        turned_lo = sem("turned_lo")
        part_b_ready = sem("part_b_ready")
        evacuated = sem("evacuated")
        scores_ready = sem("scores_ready")
        max_ready = sem("max_ready")
        exp_done = sem("exp_done")
        probs_ready = sem("probs_ready")
        probs_turned = sem("probs_turned")
        probsT_ready = sem("probsT_ready")
        pv_done = sem("pv_done")
        att_ready = sem("att_ready")
        pads_zero = sem("pads_zero")
        pooled_ready = sem("pooled_ready")
        mixed = sem("mixed")
        gate_exp = sem("gate_exp")
        y_ready = sem("y_ready")
        y_hi = sem("y_hi")
        y_lo = sem("y_lo")
        summed = sem("summed")
        sq_done = sem("sq_done")
        weighted = sem("weighted")
        half_used = sem("half_used")
        ms2_ready = sem("ms2_ready")
        rstd2_ready = sem("rstd2_ready")
        finished_dve = sem("finished_dve")
        finished_act = sem("finished_act")
        stored = sem("stored")
        dve_self = sem("dve_self")

        def pieces_of(w):
            return w.rearrange("(a t p) (g c) -> g a p t c", t=TPP, p=P, c=COLS)

        kv_dram, in_dram, out_w_dram = pieces_of(w_mem_kv[0]), pieces_of(w_in[0]), pieces_of(w_out[0])
        mem_dram = mem[0].rearrange("(h p) d -> h p d", p=P)
        x_dram = x[0].rearrange("(h p) d -> h p d", p=P)
        out_dram = out[0].rearrange("(h p) d -> h p d", p=P)

        def bank0(g):
            return 4 * (g % 2)

        def halves_of(n):
            if n >= LAST * PPG + SPLIT:
                e = n - LAST * PPG - SPLIT
                return w_end[:, e, 0], w_end[:, e, 1]
            return w_hi[:, n % SPLIT], w_lo[:, n % SPLIT]

        block = ctx.enter_context(nc.Block())

        @block.sync
        def _(sp):
            for h in range(TH):
                sp.dma_start(mem_nat[:, h], mem_dram[h]).then_inc(mem_landed[h], 16)
            for a in range(PPG):
                sp.dma_start(w_raw[:, a], kv_dram[0, a]).then_inc(landed[a], 16)
                if a == 3:
                    for h in range(TH):
                        sp.dma_start(x_nat[:, h], x_dram[h]).then_inc(x_landed[h], 16)
            for a in range(PPG):
                sp.wait_ge(lo_done, a + 1)
                sp.dma_start(w_raw[:, a], kv_dram[1, a]).then_inc(landed[a], 16)
            with sp.Fori(0, OUT0 - Q0) as g:
                for a in range(PPG):
                    sp.wait_ge(lo_done, g * PPG + (PPG + a + 1))
                    sp.dma_start(w_raw[:, a], in_dram[bass.ds(g, 1), a].rearrange("g p t c -> p (g t) c")
                                 ).then_inc(landed[a], 16)
            with sp.Fori(0, GROUPS - OUT0) as g:
                for a in range(PPG):
                    sp.wait_ge(lo_done, g * PPG + ((OUT0 - 1) * PPG + a + 1))
                    sp.dma_start(w_raw[:, a], out_w_dram[bass.ds(g, 1), a].rearrange("g p t c -> p (g t) c")
                                 ).then_inc(landed[a], 16)
            for h in range(TH):
                sp.wait_ge(finished_dve, h + 1)
                sp.dma_start(out_dram[h, :, 0:D // 2], x_res[:, h, 0:D // 2]).then_inc(stored, 16)
                sp.wait_ge(finished_act, 2 * (h + 1))
                sp.dma_start(out_dram[h, :, D // 2:D - COLS],
                             x_res[:, h, D // 2:D - COLS]).then_inc(stored, 16)
                sp.dma_start(out_dram[h, :, D - COLS:], end_scaled[:, h]).then_inc(stored, 16)
            sp.wait_ge(stored, 16 * 3 * TH)

        @block.gpsimd
        def _(pool):
            pool.memset(ident[:, :], 0.0).then_inc(pool_self, 1)
            pool.memset(mask[:, :], 0.0).then_inc(pool_self, 1)
            pool.memset(power[:, :], -0.5).then_inc(consts_ready, 1)
            pool.wait_ge(pool_self, 2)
            pool.affine_select(out=ident[:, :], in_=ident[:, :], compare_op=ALU.not_equal, fill=1.0, base=0,
                               pattern=[[-1, P]], channel_multiplier=1).then_inc(consts_ready, 1)
            pool.affine_select(out=mask[:, :], in_=mask[:, :], compare_op=ALU.is_ge, fill=MASKED, base=0,
                               pattern=[[-1, P]], channel_multiplier=1).then_inc(consts_ready, 1)
            for t in range(WINDOWS[-1]):
                pool.memset(inv_cnt[:, :, t:t + 1], 1.0 / (t + 1)).then_inc(pool_self, 1)
            pool.wait_ge(pool_self, 2 + WINDOWS[-1])
            for i, w in enumerate(WINDOWS):
                pool.memset(inv_cnt[:, i, w - 1:], 1.0 / w).then_inc(consts_ready, 1)
            for i in range(2):
                pool.wait_ge(ms_ready, i + 1)
                pool.tensor_tensor(rstd_in[:, i], ms_in[:, i], power[:, :], ALU.pow).then_inc(rstd_ready, 1)
            pool.wait_ge(pv_done, 4)
            for buf in (u_pad, sum_a, sum_b):
                pool.memset(buf[:, :, 0:PAD], 0.0).then_inc(pads_zero, 1)
            pool.wait_ge(fg_landed, 16)
            for g in range(OUT0, LAST):
                c = (g - OUT0) * COLS
                pool.wait_ge(sq_done, TH * (g - OUT0 + 1))
                for h in range(TH):
                    pool.tensor_tensor(x_res[:, h, c:c + COLS], x_res[:, h, c:c + COLS], fg[:, c:c + COLS],
                                       ALU.mult).then_inc(weighted, 1)
            for h in range(TH):
                pool.wait_ge(ms2_ready, h + 1)
                pool.tensor_tensor(rstd[:, h:h + 1], ms[:, h:h + 1], power[:, 0:1], ALU.pow).then_inc(rstd2_ready, 1)

        @block.tensor
        def _(pe):
            def turn_input(nat, i, kts, bank):
                for n, kt in enumerate(kts):
                    for h in range(TH):
                        c = (n % 2) * S + h * P
                        t = pe.transpose(ps[:, bank + n // 2, c:c + P], nat[:, h, kt * P:(kt + 1) * P], ident[:, :])
                    if n % 2:
                        t.then_inc(turned, 1)

            def rows_are_features(n, moving):
                hi, lo = halves_of(n)
                g, a = divmod(n, PPG)
                for t in range(TPP):
                    kt = a * TPP + t
                    for f in range(NF):
                        acc = ps[:, bank0(g) + f, :]
                        pe.matmul(acc, hi[:, t, f * P:(f + 1) * P], moving[:, kt], start=(kt == 0),
                                  stop=(kt == KT - 1), skip_group_check=True)
                        m = pe.matmul(acc[:, 0:S], lo[:, t, f * P:(f + 1) * P], moving[:, kt, 0],
                                      start=False, stop=(kt == KT - 1), skip_group_check=True)
                m.then_inc(piece_used, 1)

            def rows_are_tokens(n, stationary, halves=range(TH)):
                hi, lo = halves_of(n)
                g, a = divmod(n, PPG)
                for t in range(TPP):
                    kt = a * TPP + t
                    for h in halves:
                        acc = ps[:, bank0(g) + h, :]
                        tok = slice(h * P, (h + 1) * P)
                        pe.matmul(acc, stationary[:, kt, 0, tok], hi[:, t, :], start=(kt == 0), stop=False)
                        pe.matmul(acc, stationary[:, kt, 0, tok], lo[:, t, :], start=False, stop=False)
                        m = pe.matmul(acc, stationary[:, kt, 1, tok], hi[:, t, :], start=False, stop=(kt == KT - 1))
                return m

            def scores(g, pair):
                for f in range(2 * pair, 2 * pair + 2):
                    b = bank0(g + 1) + f
                    if g == MEM_JOB:
                        for h in range(TH):
                            m = pe.matmul(ps[:, b, h * M:(h + 1) * M], qmT[:, f, h * P:(h + 1) * P], mkT[:, f, :],
                                          start=True, stop=True)
                    else:
                        head = NF * CAUSAL_JOBS[g] + f
                        pe.matmul(ps[:, b, 0:P], qT[:, head, 0:P], kT[:, head, 0:P], start=True, stop=True)
                        m = pe.matmul(ps[:, b, P:P + S], qT[:, head, P:S], kT[:, head, :], start=True, stop=True)
                m.then_inc(scores_ready, 1)

            def turn_probs(g, pair):
                pe.wait_ge(probs_ready, 2 * JOBS.index(g) + pair + 1)
                for f in range(2 * pair, 2 * pair + 2):
                    b = bank0(g + 1) + f
                    if g == MEM_JOB:
                        for h in range(TH):
                            for k in range(TH):
                                m = pe.transpose(ps[:, b, k * S + h * P:k * S + (h + 1) * P],
                                                 probs_end[:, f, h * M + k * P:h * M + (k + 1) * P], ident[:, :])
                    else:
                        for c in range(3):
                            m = pe.transpose(ps[:, b, c * P:(c + 1) * P], probs[:, f, c * P:(c + 1) * P], ident[:, :])
                m.then_inc(probs_turned, 1)

            def weigh_values(g, pair):
                pe.wait_ge(probsT_ready, 2 * JOBS.index(g) + pair + 1)
                for f in range(2 * pair, 2 * pair + 2):
                    b = bank0(g + 1) + f
                    if g == MEM_JOB:
                        for k in range(TH):
                            m = pe.matmul(ps[:, b, 0:S], mv[:, k, f * HD:(f + 1) * HD],
                                          probs_end[:, NF + f, k * S:(k + 1) * S], start=(k == 0), stop=(k == 1))
                    else:
                        c = (NF * CAUSAL_JOBS[g] + f) * HD
                        pe.matmul(ps[:, b, 0:S], v[:, 0, c:c + HD], probsT[:, f, 0:S], start=True, stop=False)
                        m = pe.matmul(ps[:, b, P:S], v[:, 1, c:c + HD], probsT[:, f, S:S + P],
                                      start=False, stop=True)
                m.then_inc(pv_done, 1)

            pe.wait_ge(rows_landed, 48)
            pe.wait_ge(consts_ready, 3)
            pe.transpose(ps[:, 4, 0:2 * KT + NF], rows[:, :], ident[0:2 * KT + NF, 0:2 * KT + NF]).then_inc(rows_turned, 1)
            pe.wait_ge(scaled, 2)
            turn_input(mem_nat, 0, range(0, 8), 0)
            pe.wait_ge(cols_ready, 1)
            turn_input(mem_nat, 0, range(8, 16), 4)

            for n in range(PIECES):
                g, a = divmod(n, PPG)
                if a == 0 and 2 <= g < OUT0 + 2:
                    pe.wait_ge(evacuated, g - 1)
                if a == 0 and g >= OUT0 + 2:
                    pe.wait_ge(summed, g - 1 - OUT0)
                if a == 0 and g - 1 in BRANCHES:
                    pe.wait_ge(att_ready, 2 * (BRANCHES.index(g - 1) + 1))
                if a == 0 and g == Q0:
                    pe.wait_ge(turned_lo, KT)
                if g == MK:
                    pe.wait_ge(turned_lo, a + 1 if a else 4)
                if g == MV and a == 0:
                    pe.wait_ge(turned_lo, KT // 2)
                if g >= OUT0 and a % 2 == 0:
                    pe.wait_ge(y_lo, min(a // 2 + 1, len(GATES)))
                pe.wait_ge(lo_done, n + 1)
                if g == LAST:
                    m = rows_are_tokens(n, yT, range(0, 1))
                    if a == PPG - 1:
                        m.then_inc(half_used, 1)
                elif g >= OUT0:
                    rows_are_tokens(n, yT).then_inc(piece_used, 1)
                elif g in TOKENS_ON_ROWS:
                    rows_are_tokens(n, memT if g == MV else xT).then_inc(piece_used, 1)
                else:
                    rows_are_features(n, memT if g == MK else xT)

                if g == MV and a in (1, 3):
                    if a == 1:
                        pe.wait_ge(evacuated, MK + 1)
                        pe.wait_ge(scaled, 4)
                    else:
                        pe.wait_ge(turned_lo, KT // 2 + 4)
                    turn_input(x_nat, 1, range(4 * (a - 1), 4 * (a - 1) + 8), 0)
                if g in JOBS:
                    if a == 0:
                        pe.wait_ge(evacuated, g)
                        scores(g, 0)
                        scores(g, 1)
                    if a == 4:
                        turn_probs(g, 0)
                    if a == 5:
                        turn_probs(g, 1)
                        weigh_values(g, 0)
                    if a == 6:
                        weigh_values(g, 1)
                if g == GP and a == 4:
                    pe.wait_ge(wp_landed, 16)
                    pe.wait_ge(pooled_ready, NF)
                    for i in range(NF):
                        m = pe.matmul(ps[:, bank0(g + 1) + i, 0:S], wp[:, i, :], u_pad[:, i, PAD:], start=True, stop=True)
                    m.then_inc(mixed, 1)
                if g == QM and a == 0:
                    pass
            for a in range(PPG):
                m = rows_are_tokens(LAST * PPG + a, yT, range(1, 2))
            m.then_inc(half_used, 1)

        @block.scalar
        def _(act):
            def split_hi(n):
                act.wait_ge(landed[n % RAW], 16 * (n // RAW + 1))
                if SPLIT <= n < LAST * PPG + SPLIT:
                    act.wait_ge(piece_used, n - SPLIT + 1)
                elif n == LAST * PPG + SPLIT:
                    act.wait_ge(piece_used, GM * PPG + PPG)
                act.activation(halves_of(n)[0], w_raw[:, n % RAW], ACT.Copy).then_inc(hi_done, 1)

            def square_input(nat, i, h, landed_sem):
                act.wait_ge(landed_sem, 16)
                if 2 * i + h:
                    act.wait_ge(squared, 2 * i + h)
                act.activation(squares[:, :], nat[:, h, :], ACT.Square,
                               accum_out=ssq_in[:, i, h:h + 1]).then_inc(squared, 1)

            def turned_to_hi(dst, i, b, bank):
                act.wait_ge(turned, KT // 2 * i + b + 1)
                for kt in (2 * b, 2 * b + 1):
                    gain = (KT if i == 0 else 0) + kt
                    m = act.activation(dst[:, kt, 0], ps[:, bank + b % 4, kt % 2 * S:(kt % 2 + 1) * S], ACT.Copy,
                                       scale=cols[:, gain:gain + 1])
                m.then_inc(turned_hi, 1)

            def exps(g, pair):
                j = 2 * JOBS.index(g) + pair
                act.wait_ge(max_ready, j + 1)
                for f in range(2 * pair, 2 * pair + 2):
                    for h in range(TH):
                        c, w = (h * M, M) if g == MEM_JOB else (h * P, P + h * P)
                        dst = probs_end if g == MEM_JOB else probs
                        m = act.activation(dst[:, f, c:c + w], ps[:, bank0(g + 1) + f, c:c + w], ACT.Exp,
                                           bias=nmax[:, f, h:h + 1], accum_out=sums[:, f, h:h + 1])
                m.then_inc(exp_done, 1)

            def copy_probsT(g, pair):
                j = 2 * JOBS.index(g) + pair
                act.wait_ge(probs_turned, j + 1)
                w = 2 * S if g == MEM_JOB else S + P
                b = bank0(g + 1) + 2 * pair
                dst = probs_end[:, NF + 2 * pair:NF + 2 * pair + 2] if g == MEM_JOB else probsT[:, 2 * pair:2 * pair + 2]
                act.activation(dst[:, :, 0:w], ps[:, b:b + 2, 0:w], ACT.Copy).then_inc(probsT_ready, 1)

            def copy_att(g, pair):
                j = JOBS.index(g)
                act.wait_ge(pv_done, 2 * j + pair + 1)
                if g == MEM_JOB:
                    act.wait_ge(y_ready, 2)
                b = bank0(g + 1) + 2 * pair
                act.activation(att[:, min(j, 1), 2 * pair:2 * pair + 2], ps[:, b:b + 2, 0:S],
                               ACT.Copy).then_inc(att_ready, 1)

            act.dma_start(rows[0:KT, :], norm_g.rearrange("a (r c) -> (a r) c", c=P)).then_inc(rows_landed, 16)
            act.dma_start(rows[KT:2 * KT, :], mem_norm_g.rearrange("a (r c) -> (a r) c", c=P)).then_inc(rows_landed, 16)
            act.dma_start(rows[2 * KT:, :], pool_scale.rearrange("a (r c) -> (a r) c", c=P)).then_inc(rows_landed, 16)
            act.dma_start(wp[:, :, :], w_pool[0].rearrange("g c d -> c g d")).then_inc(wp_landed, 16)

            for h in range(TH):
                square_input(mem_nat, 0, h, mem_landed[h])
            split_hi(0)
            act.wait_ge(cols_ready, 1)
            for b in range(KT // 2):
                turned_to_hi(memT, 0, b, 4 * (b // 4))
                if b in (1, 3, 5):
                    split_hi(b // 2 + 1)

            for n in range(PIECES):
                g, a = divmod(n, PPG)
                if a == PPG - 1 and g < OUT0 and g not in TOKENS_ON_ROWS:
                    act.wait_ge(piece_used, n + 1)
                    if g >= 1:
                        act.wait_ge(evacuated, g)
                    if g - 1 in GATES:
                        act.wait_ge(y_ready, GATES.index(g - 1) + 1)
                    act.activation(part_b[:, :, :], ps[:, bank0(g):bank0(g) + NF, S:2 * S], ACT.Copy,
                                   scale=SCALE if g in (Q0, Q1, QM) else 1.0).then_inc(part_b_ready, 1)
                if n + SPLIT < PIECES:
                    split_hi(n + SPLIT)
                if g == MK and a in (2, 3):
                    square_input(x_nat, 1, a - 2, x_landed[a - 2])
                if g == MV and a in (1, 3):
                    for b in range(2 * (a - 1), 2 * (a - 1) + 4):
                        turned_to_hi(xT, 1, b, 0)
                if g in JOBS:
                    if a == 0:
                        exps(g, 0)
                        exps(g, 1)
                    if a == 4:
                        copy_probsT(g, 0)
                    if a == 5:
                        copy_probsT(g, 1)
                        copy_att(g, 0)
                    if a == 6:
                        copy_att(g, 1)
                if g == GA1 and a == 2:
                    act.wait_ge(scores_ready, 4)
                    for h in range(TH):
                        act.dma_start(x_res[:, h], x_dram[h]).then_inc(res_landed, 16)
                    act.dma_start(fg[:, :], final_g.rearrange("(a d) -> a d", a=1).partition_broadcast(P)
                                  ).then_inc(fg_landed, 16)
                if g == GP and a == 4:
                    act.wait_ge(mixed, 1)
                    act.wait_ge(y_ready, 1)
                    for i in range(NF):
                        m = act.activation(att[:, 0, i], ps[:, bank0(g + 1) + i, 0:S], ACT.Copy,
                                           scale=cols[:, 2 * KT + i:2 * KT + i + 1])
                        if i % 2:
                            m.then_inc(att_ready, 1)
                if g - 1 in GATES:
                    i = GATES.index(g - 1)
                    if a == 1:
                        act.wait_ge(evacuated, g)
                        act.activation(part_b[:, :, :], gate[:, :, :], ACT.Exp, scale=-1.0).then_inc(gate_exp, 1)
                    if a == 3:
                        act.wait_ge(y_ready, i + 1)
                        act.activation(yT[:, NF * i:NF * (i + 1), 0], gate[:, :, :], ACT.Copy).then_inc(y_hi, 1)
                if OUT0 <= g < LAST and a == PPG - 1:
                    c = (g - OUT0) * COLS
                    act.wait_ge(summed, g - OUT0 + 1)
                    for h in range(TH):
                        act.wait_ge(sq_done, TH * (g - OUT0) + h) if g > OUT0 or h else None
                        act.activation(squares[:, 0:COLS], x_res[:, h, c:c + COLS], ACT.Square,
                                       accum_out=ssq[:, h, g - OUT0:g - OUT0 + 1]).then_inc(sq_done, 1)
            for h in range(TH):
                act.wait_ge(summed, LAST - OUT0 + h + 1)
                act.wait_ge(sq_done, TH * (LAST - OUT0) + h)
                act.activation(squares[:, 0:COLS], x_res[:, h, D - COLS:], ACT.Square,
                               accum_out=ssq[:, h, LAST - OUT0:]).then_inc(sq_done, 1)
                act.wait_ge(rstd2_ready, h + 1)
                act.wait_ge(weighted, TH * (LAST - OUT0))
                act.activation(end_scaled[:, h], end_scaled[:, h], ACT.Copy, scale=rstd[:, h:h + 1]).then_inc(finished_act, 1)
                act.activation(x_res[:, h, D // 2:D - COLS], x_res[:, h, D // 2:D - COLS], ACT.Copy,
                               scale=rstd[:, h:h + 1]).then_inc(finished_act, 1)

        @block.vector
        def _(dve):
            steps = [0]

            def settle(ins):
                steps[0] += 1
                ins.then_inc(dve_self, 1)
                dve.wait_ge(dve_self, steps[0])

            def split_lo(n):
                hi, lo = halves_of(n)
                dve.wait_ge(hi_done, n + 1)
                dve.tensor_tensor(lo, w_raw[:, n % RAW], hi.bitcast(F32), ALU.subtract).then_inc(lo_done, 1)

            def rms_input(nat, i):
                dve.wait_ge(squared, 2 * i + 2)
                dve.tensor_scalar(ms_in[:, i], ssq_in[:, i], 1.0 / D, EPS, ALU.mult, ALU.add).then_inc(ms_ready, 1)
                dve.wait_ge(rstd_ready, i + 1)
                for h in range(TH):
                    dve.tensor_scalar(nat[:, h, :], nat[:, h, :], rstd_in[:, i, h:h + 1], None,
                                      ALU.mult).then_inc(scaled, 1)

            def turned_to_lo(dst, i, b, bank):
                dve.wait_ge(turned_hi, KT // 2 * i + b + 1)
                for kt in (2 * b, 2 * b + 1):
                    gain = (KT if i == 0 else 0) + kt
                    m = dve.scalar_tensor_tensor(out=dst[:, kt, 1], in0=ps[:, bank + b % 4, kt % 2 * S:(kt % 2 + 1) * S],
                                                 scalar=cols[:, gain:gain + 1], in1=dst[:, kt, 0].bitcast(F32),
                                                 op0=ALU.mult, op1=ALU.subtract)
                m.then_inc(turned_lo, 1)

            def evacuate(g):
                if g in TOKENS_ON_ROWS:
                    dst = {MV: mv[:, :, :], V0: v[:, :, 0:COLS], V1: v[:, :, COLS:]}[g]
                    dve.tensor_copy(dst, ps[:, bank0(g):bank0(g) + TH, :]).then_inc(evacuated, 1)
                    return
                dst = {MK: mkT, QM: qmT, Q0: qT[:, 0:NF], Q1: qT[:, NF:], K0: kT[:, 0:NF], K1: kT[:, NF:],
                       U: u_pad[:, :, PAD:]}.get(g, gate)
                dve.wait_ge(part_b_ready, sum(i not in TOKENS_ON_ROWS for i in range(g + 1)))
                if g in GATES and g != GA0:
                    dve.wait_ge(y_lo, GATES.index(g))
                hi_part = ps[:, bank0(g):bank0(g) + NF, 0:S]
                for f in range(0, NF, NF):
                    dve.scalar_tensor_tensor(out=dst[:, :, :], in0=hi_part, scalar=SCALE if g in (Q0, Q1, QM) else 1.0,
                                             in1=part_b[:, :, :], op0=ALU.mult, op1=ALU.add).then_inc(evacuated, 1)

            def mask_and_max(g, pair):
                j = 2 * JOBS.index(g) + pair
                dve.wait_ge(scores_ready, j + 1)
                b = bank0(g + 1) + 2 * pair
                own = slice(2 * pair, 2 * pair + 2)
                if g == MEM_JOB:
                    dve.tensor_reduce(nmax[:, own, :], ps[:, b:b + 2, :].rearrange("p f (h k) -> p f h k", h=TH),
                                      AX.X, ALU.max, negate=True).then_inc(max_ready, 1)
                    return
                diag = ps[:, b:b + 2, :].rearrange("p f (h k) -> p f h k", h=TH)[:, :, :, 0:P]
                settle(dve.tensor_tensor(diag, diag, mask[:, :].rearrange("p (f h k) -> p f h k", f=1, h=1)
                                         .to_broadcast([P, 2, TH, P]), ALU.add))
                dve.tensor_reduce(nmax[:, own, 0:1], ps[:, b:b + 2, 0:P], AX.X, ALU.max, negate=True)
                dve.tensor_reduce(nmax[:, own, 1:2], ps[:, b:b + 2, P:P + S], AX.X, ALU.max,
                                  negate=True).then_inc(max_ready, 1)

            def normalise(g, pair):
                j = 2 * JOBS.index(g) + pair
                dve.wait_ge(exp_done, j + 1)
                own = slice(2 * pair, 2 * pair + 2)
                settle(dve.reciprocal(rsum[:, own, :], sums[:, own, :]))
                for h in range(TH):
                    c, w = (h * M, M) if g == MEM_JOB else (h * P, P + h * P)
                    part = (probs_end if g == MEM_JOB else probs)[:, own, c:c + w]
                    m = dve.tensor_tensor(part, part, rsum[:, own, h:h + 1].to_broadcast([P, 2, w]), ALU.mult)
                m.then_inc(probs_ready, 1)

            def pool_windows():
                dve.wait_ge(evacuated, U + 1)
                dve.wait_ge(pads_zero, 3)
                dve.wait_ge(consts_ready, 3 + NF)
                src = u_pad
                for i in range(NF):
                    dst, sh = (sum_a, sum_b)[i % 2], 1 << i
                    settle(dve.tensor_tensor(dst[:, i:, PAD:], src[:, i:, PAD:], src[:, i:, PAD - sh:PAD - sh + S],
                                             ALU.add))
                    src = dst
                for i, w in enumerate(WINDOWS):
                    total = (sum_a, sum_b)[i % 2]
                    first = slice(PAD, PAD + WINDOWS[-1])
                    rest = slice(PAD + WINDOWS[-1], PAD + S)
                    settle(dve.tensor_tensor(total[:, i, first], total[:, i, first], inv_cnt[:, i, :], ALU.mult))
                    settle(dve.tensor_tensor(u_pad[:, i, first], total[:, i, first], u_pad[:, i, first], ALU.subtract))
                    dve.scalar_tensor_tensor(out=u_pad[:, i, rest], in0=total[:, i, rest], scalar=1.0 / w,
                                             in1=u_pad[:, i, rest], op0=ALU.mult, op1=ALU.subtract
                                             ).then_inc(pooled_ready, 1)

            dve.wait_ge(rows_turned, 1)
            dve.tensor_copy(cols[:, :], ps[:, 4, 0:2 * KT + NF]).then_inc(cols_ready, 1)
            rms_input(mem_nat, 0)
            split_lo(0)
            for b in range(KT // 2):
                turned_to_lo(memT, 0, b, 4 * (b // 4))
                if b in (1, 3, 5):
                    split_lo(b // 2 + 1)

            for n in range(PIECES):
                g, a = divmod(n, PPG)
                if a == PPG - 1 and g < OUT0:
                    dve.wait_ge(piece_used, n + 1)
                    evacuate(g)
                if n + SPLIT < PIECES:
                    split_lo(n + SPLIT)
                if g == MK and a == 3:
                    rms_input(x_nat, 1)
                if g == MV and a in (1, 3):
                    for b in range(2 * (a - 1), 2 * (a - 1) + 4):
                        turned_to_lo(xT, 1, b, 0)
                if g in JOBS:
                    if a == 0:
                        mask_and_max(g, 0)
                        mask_and_max(g, 1)
                    if a == 1:
                        normalise(g, 0)
                    if a == 2:
                        normalise(g, 1)
                if g == GP and a == 0:
                    pool_windows()
                if g - 1 in GATES:
                    i = GATES.index(g - 1)
                    if a == 2:
                        dve.wait_ge(gate_exp, i + 1)
                        settle(dve.tensor_scalar(part_b[:, :, :], part_b[:, :, :], 1.0, None, ALU.add))
                        settle(dve.reciprocal(part_b[:, :, :], part_b[:, :, :]))
                        settle(dve.tensor_tensor(gate[:, :, :], gate[:, :, :], part_b[:, :, :], ALU.mult))
                        dve.wait_ge(att_ready, 2 * (i + 1))
                        dve.tensor_tensor(gate[:, :, :], gate[:, :, :], att[:, i % 2], ALU.mult).then_inc(y_ready, 1)
                    if a == 3:
                        dve.wait_ge(y_hi, i + 1)
                        own = slice(NF * i, NF * (i + 1))
                        dve.tensor_tensor(yT[:, own, 1], gate[:, :, :], yT[:, own, 0].bitcast(F32),
                                          ALU.subtract).then_inc(y_lo, 1)
                if OUT0 <= g < LAST and a == PPG - 1:
                    dve.wait_ge(piece_used, n + 1)
                    if g == OUT0:
                        dve.wait_ge(res_landed, 16 * TH)
                    c = (g - OUT0) * COLS
                    dve.tensor_tensor(x_res[:, :, c:c + COLS], ps[:, bank0(g):bank0(g) + TH, :],
                                      x_res[:, :, c:c + COLS], ALU.add).then_inc(summed, 1)
            for h in range(TH):
                dve.wait_ge(half_used, h + 1)
                dve.tensor_tensor(x_res[:, h, D - COLS:], ps[:, bank0(LAST) + h, :], x_res[:, h, D - COLS:],
                                  ALU.add).then_inc(summed, 1)
                dve.wait_ge(summed, LAST - OUT0 + h + 1)
                dve.wait_ge(fg_landed, 16)
                dve.tensor_tensor(end_scaled[:, h], x_res[:, h, D - COLS:], fg[:, D - COLS:], ALU.mult)
                dve.wait_ge(sq_done, TH * (LAST - OUT0) + h + 1)
                settle(dve.tensor_reduce(sst[:, h:h + 1], ssq[:, h, :], AX.X, ALU.add))
                dve.tensor_scalar(ms[:, h:h + 1], sst[:, h:h + 1], 1.0 / D, EPS, ALU.mult, ALU.add).then_inc(ms2_ready, 1)
                dve.wait_ge(rstd2_ready, h + 1)
                dve.wait_ge(weighted, TH * (LAST - OUT0))
                dve.tensor_scalar(x_res[:, h, 0:D // 2], x_res[:, h, 0:D // 2], rstd[:, h:h + 1], None,
                                  ALU.mult).then_inc(finished_dve, 1)


_INS = ["x", "mem", "norm_g", "mem_norm_g", "w_in", "w_mem_kv", "w_pool", "pool_scale", "w_out", "final_norm_g"]


def kernel(**inputs):
    import numpy as _np
    import concourse.bacc as _bacc
    from concourse import mybir as _mybir
    from concourse.bass_utils import run_bass_kernel_spmd as _run

    nc = _bacc.Bacc("TRN2", target_bir_lowering=False, num_devices=1)
    arrays, args = {}, []
    for name in _INS:
        a = _np.ascontiguousarray(inputs[name])
        arrays[f"in_{name}"] = a
        args.append(nc.dram_tensor(f"in_{name}", a.shape, _mybir.dt.from_np(a.dtype), kind="ExternalInput").ap())
    args.append(nc.dram_tensor("out_0", (1, S, D), F32, kind="ExternalOutput").ap())
    build(nc, *args)
    r = _run(nc, [arrays], core_ids=[0])
    return r.results[0]["out_0"]
```

```python
from contextlib import ExitStack

import concourse.bass as bass
from concourse import mybir

F32 = mybir.dt.float32
F32R = mybir.dt.float32r
ALU = mybir.AluOpType
ACT = mybir.ActivationFunctionType
AX = mybir.AxisListType

P = 128
D = 2048
S = 256
M = 256
HD = 128
KT = D // P
COLS = 512
NF = COLS // P
TH = S // P
EPS = 1e-6
SCALE = HD ** -0.5
WINDOWS = (2, 4, 8, 16)
PAD = WINDOWS[-1] // 2
MASKED = -3.0e38

WARM_UP = 12
MEM_BLOCKS = 4
TPP = 2
PPG = KT // TPP
RAW = 8
SPLIT = 4

(MK, MV, Q0, Q1, K0, K1, V0, V1, GA0, GA1, U, GP, QM, GM, OUT0) = range(15)
GROUPS = OUT0 + D // COLS
LAST = GROUPS - 1
PIECES = GROUPS * PPG
TOKENS_ON_ROWS = (MV, V0, V1)
CAUSAL_JOBS = {V1: 0, GA0: 1}
MEM_JOB = GM
JOBS = (V1, GA0, GM)
FACTOR = {Q0: SCALE, Q1: SCALE, QM: SCALE, GA0: 0.5, GA1: 0.5, GP: 0.5, GM: 0.5}
BRANCHES = (V1, GA0, GP, GM)
GATES = (GA0, GA1, GP, GM)


def build(nc, x, mem, norm_g, mem_norm_g, w_in, w_mem_kv, w_pool, pool_scale, w_out, final_g, out):
    with ExitStack() as ctx:
        def sb(name, shape, dt=F32, stack=ctx):
            return stack.enter_context(nc.sbuf_tensor(name, shape, dt))

        def sem(name):
            return ctx.enter_context(nc.semaphore(name))

        w_raw = sb("w_raw", [P, RAW, TPP, COLS])
        w_hi = sb("w_hi", [P, SPLIT, TPP, COLS], F32R)
        w_lo = sb("w_lo", [P, SPLIT, TPP, COLS], F32R)
        early = ExitStack()
        xT = sb("xT", [P, KT, 2, S], F32R, early)
        early.close()
        w_end = sb("w_end", [P, SPLIT, 2, TPP, COLS], F32R)
        early = ExitStack()
        mem_nat = sb("mem_nat", [P, TH, D], F32, early)
        x_nat = sb("x_nat", [P, TH, D], F32, early)
        early.close()
        yT = sb("yT", [P, KT, 2, S], F32R)
        early = ExitStack()
        memT = sb("memT", [P, KT, 2, S], F32R, early)
        early.close()
        early = ExitStack()
        qT = sb("qT", [P, 2 * NF, S], F32, early)
        kT = sb("kT", [P, 2 * NF, S], F32, early)
        early.close()
        x_res = sb("x_res", [P, TH, D])
        early = ExitStack()
        qmT = sb("qmT", [P, NF, S], F32, early)
        early.close()
        v = sb("v", [P, TH, 2 * COLS])
        fg = sb("fg", [P, D])
        mkT = sb("mkT", [P, NF, S])
        mv = sb("mv", [P, TH, COLS])
        early = ExitStack()
        probs = sb("probs", [P, NF, 2 * S], F32, early)
        probsT = sb("probsT", [P, NF, 2 * S], F32, early)
        early.close()
        early = ExitStack()
        u_pad = sb("u_pad", [P, NF, PAD + S], F32, early)
        sum_a = sb("sum_a", [P, NF, PAD + S], F32, early)
        sum_b = sb("sum_b", [P, NF, PAD + S], F32, early)
        early.close()
        early = ExitStack()
        squares = sb("squares", [P, D], F32, early)
        kept = ExitStack()
        diag = sb("diag", [P, TH, P], F32, kept)
        mem_rstd = sb("mem_rstd", [P, 1, M], F32, kept)
        kept.close()
        end_scaled = sb("end_scaled", [P, TH, COLS], F32, early)
        early.close()
        probs_end = sb("probs_end", [P, 2 * NF, 2 * S])
        att = sb("att", [P, 2, NF, S])
        part_b = sb("part_b", [P, NF, S])
        gate = sb("gate", [P, NF, S])
        ident = sb("ident", [P, P])
        mask = sb("mask", [P, P])
        ones = sb("ones", [P, P])
        rows = sb("rows", [2 * KT + NF, P])
        cols = sb("cols", [P, 2 * KT + NF])
        wp = sb("wp", [P, NF, P])
        inv_cnt = sb("inv_cnt", [P, NF, WINDOWS[-1]])
        nmax = sb("nmax", [P, NF, 2])
        sums = sb("sums", [P, NF, 2])
        rsum = sb("rsum", [P, NF, 2])
        ssq_in = sb("ssq_in", [P, 2, TH])
        ms_in = sb("ms_in", [P, 2, TH])
        rstd_in = sb("rstd_in", [P, 2, TH])
        ssq = sb("ssq", [P, TH, D // COLS])
        sst = sb("sst", [P, TH])
        ms = sb("ms", [P, TH])
        rstd = sb("rstd", [P, TH])
        power = sb("power", [P, 2])

        ps = ctx.enter_context(nc.psum_tensor("ps", [P, 8, 512], F32))

        landed = [sem(f"landed{i}") for i in range(RAW)]
        rows_landed = sem("rows_landed")
        wp_landed = sem("wp_landed")
        mem_landed = [sem(f"mem_landed{i}") for i in range(MEM_BLOCKS)]
        x_landed = [sem(f"x_landed{i}") for i in range(TH)]
        fg_landed = sem("fg_landed")
        res_landed = sem("res_landed")
        hi_done = sem("hi_done")
        lo_done = sem("lo_done")
        piece_used = sem("piece_used")
        consts_ready = sem("consts_ready")
        ones_ready = sem("ones_ready")
        pool_self = sem("pool_self")
        rows_turned = sem("rows_turned")
        cols_ready = sem("cols_ready")
        squared = sem("squared")
        ms_ready = sem("ms_ready")
        rstd_ready = sem("rstd_ready")
        table_loaded = sem("table_loaded")
        scaled = sem("scaled")
        diag_ready = sem("diag_ready")
        spread = sem("spread")
        spread_read = sem("spread_read")
        mk_scaled = sem("mk_scaled")
        turned = sem("turned")
        turned_hi = sem("turned_hi")
        turned_lo = sem("turned_lo")
        part_b_ready = sem("part_b_ready")
        evacuated = sem("evacuated")
        scores_ready = sem("scores_ready")
        max_ready = sem("max_ready")
        exp_done = sem("exp_done")
        probs_ready = sem("probs_ready")
        probs_turned = sem("probs_turned")
        probsT_ready = sem("probsT_ready")
        pv_done = sem("pv_done")
        att_ready = sem("att_ready")
        pads_zero = sem("pads_zero")
        pooled_ready = sem("pooled_ready")
        mixed = sem("mixed")
        gate_tanh = sem("gate_tanh")
        gate_att = sem("gate_att")
        y_ready = sem("y_ready")
        y_hi = sem("y_hi")
        y_lo = sem("y_lo")
        summed = sem("summed")
        sq_done = sem("sq_done")
        weighted = sem("weighted")
        half_used = sem("half_used")
        ms2_ready = sem("ms2_ready")
        rstd2_ready = sem("rstd2_ready")
        finished_dve = sem("finished_dve")
        finished_act = sem("finished_act")
        stored = sem("stored")
        dve_self = sem("dve_self")

        def pieces_of(w):
            return w.rearrange("(a t p) (g c) -> g a p t c", t=TPP, p=P, c=COLS)

        kv_dram, in_dram, out_w_dram = pieces_of(w_mem_kv[0]), pieces_of(w_in[0]), pieces_of(w_out[0])
        x_dram = x[0].rearrange("(h p) d -> h p d", p=P)
        out_dram = out[0].rearrange("(h p) d -> h p d", p=P)

        def bank0(g):
            return 4 * (g % 2)

        def halves_of(n):
            if LAST * PPG <= n < LAST * PPG + SPLIT:
                return w_end[:, n % SPLIT, 0], w_end[:, n % SPLIT, 1]
            return w_hi[:, n % SPLIT], w_lo[:, n % SPLIT]

        def pieces_to_split(n):
            ahead = n - (LAST * PPG - SPLIT)
            if ahead < 0:
                return range(n + SPLIT, n + SPLIT + 1)
            return range(min(n + SPLIT + ahead, PIECES), min(n + SPLIT + ahead + 2, PIECES))

        block = ctx.enter_context(nc.Block())

        @block.sync
        def _(sp):
            for a in range(PPG):
                if a < MEM_BLOCKS:
                    c = slice(a * (D // MEM_BLOCKS), (a + 1) * (D // MEM_BLOCKS))
                    sp.dma_start(mem_nat[:, :, c], mem[0, :, c].rearrange("(h p) d -> p h d", p=P)).then_inc(mem_landed[a], 16)
                sp.dma_start(w_raw[:, a], kv_dram[0, a]).then_inc(landed[a], 16)
                if a in (5, 6):
                    sp.dma_start(x_nat[:, a - 5], x_dram[a - 5]).then_inc(x_landed[a - 5], 16)
            sp.dma_start(wp[:, :, :], w_pool[0].rearrange("g c d -> c g d")).then_inc(wp_landed, 16)
            for a in range(PPG):
                sp.wait_ge(lo_done, a + 1)
                sp.dma_start(w_raw[:, a], kv_dram[1, a]).then_inc(landed[a], 16)
            with sp.Fori(0, OUT0 - Q0) as g:
                for a in range(PPG):
                    sp.wait_ge(lo_done, g * PPG + (PPG + a + 1))
                    sp.dma_start(w_raw[:, a], in_dram[bass.ds(g, 1), a].rearrange("g p t c -> p (g t) c")
                                 ).then_inc(landed[a], 16)
            with sp.Fori(0, GROUPS - OUT0) as g:
                for a in range(PPG):
                    sp.wait_ge(lo_done, g * PPG + ((OUT0 - 1) * PPG + a + 1))
                    sp.dma_start(w_raw[:, a], out_w_dram[bass.ds(g, 1), a].rearrange("g p t c -> p (g t) c")
                                 ).then_inc(landed[a], 16)
            for h in range(TH):
                for i in range(3):
                    c = slice(i * COLS, (i + 1) * COLS)
                    sp.wait_ge(finished_dve, 3 * h + i + 1)
                    sp.dma_start(out_dram[h, :, c], x_res[:, h, c]).then_inc(stored, 16)
                sp.wait_ge(finished_act, h + 1)
                sp.dma_start(out_dram[h, :, D - COLS:], end_scaled[:, h]).then_inc(stored, 16)
            sp.wait_ge(stored, 16 * 4 * TH)

        @block.gpsimd
        def _(pool):
            pool.memset(ones[:, :], 1.0).then_inc(ones_ready, 1)
            pool.memset(ident[:, :], 0.0).then_inc(pool_self, 1)
            pool.memset(mask[:, :], 0.0).then_inc(pool_self, 1)
            pool.memset(power[:, :], -0.5).then_inc(consts_ready, 1)
            pool.wait_ge(pool_self, 2)
            pool.affine_select(out=ident[:, :], in_=ident[:, :], compare_op=ALU.not_equal, fill=1.0, base=0,
                               pattern=[[-1, P]], channel_multiplier=1).then_inc(consts_ready, 1)
            pool.affine_select(out=mask[:, :], in_=mask[:, :], compare_op=ALU.is_ge, fill=MASKED, base=0,
                               pattern=[[-1, P]], channel_multiplier=1).then_inc(consts_ready, 1)
            for t in range(WINDOWS[-1]):
                pool.memset(inv_cnt[:, :, t:t + 1], 1.0 / (t + 1)).then_inc(pool_self, 1)
            pool.wait_ge(pool_self, 2 + WINDOWS[-1])
            for i, w in enumerate(WINDOWS):
                pool.memset(inv_cnt[:, i, w - 1:], 1.0 / w).then_inc(consts_ready, 1)
            for i in range(2):
                pool.wait_ge(ms_ready, i + 1)
                pool.tensor_tensor(rstd_in[:, i], ms_in[:, i], power[:, :], ALU.pow).then_inc(rstd_ready, 1)
            pool.wait_ge(evacuated, MK + 1)
            pool.wait_ge(spread_read, 1)
            pool.tensor_tensor(mkT[:, :, :], mkT[:, :, :], mem_rstd[:, :, :].to_broadcast([P, NF, M]),
                               ALU.mult).then_inc(mk_scaled, 1)
            pool.wait_ge(pv_done, 4)
            for buf in (u_pad, sum_a, sum_b):
                pool.memset(buf[:, :, 0:PAD], 0.0).then_inc(pads_zero, 1)
            for i, g in enumerate(GATES):
                pool.wait_ge(gate_tanh, i + 1)
                pool.wait_ge(att_ready, 2 * (i + 1))
                pool.tensor_tensor(gate[:, :, :], gate[:, :, :], att[:, i % 2], ALU.mult).then_inc(gate_att, 1)
            pool.wait_ge(fg_landed, 16)
            for g in range(OUT0, LAST):
                c = (g - OUT0) * COLS
                pool.wait_ge(sq_done, TH * (g - OUT0 + 1))
                for h in range(TH):
                    pool.tensor_tensor(x_res[:, h, c:c + COLS], x_res[:, h, c:c + COLS], fg[:, c:c + COLS],
                                       ALU.mult).then_inc(weighted, 1)
            for h in range(TH):
                pool.wait_ge(ms2_ready, h + 1)
                pool.tensor_tensor(rstd[:, h:h + 1], ms[:, h:h + 1], power[:, 0:1], ALU.pow).then_inc(rstd2_ready, 1)

        @block.tensor
        def _(pe):
            def turn_input(nat, i, kts, bank):
                for kt in kts:
                    for h in range(TH):
                        c = kt % 2 * S + h * P
                        t = pe.transpose(ps[:, bank + kt // 2 % 4, c:c + P], nat[:, h, kt * P:(kt + 1) * P], ident[:, :])
                    if kt % 2:
                        t.then_inc(turned, 1)

            def rows_are_features(n, moving):
                hi, lo = halves_of(n)
                g, a = divmod(n, PPG)
                for t in range(TPP):
                    kt = a * TPP + t
                    for f in range(NF):
                        acc = ps[:, bank0(g) + f, :]
                        pe.matmul(acc, hi[:, t, f * P:(f + 1) * P], moving[:, kt], start=(kt == 0),
                                  stop=(kt == KT - 1), skip_group_check=True)
                        m = pe.matmul(acc[:, 0:S], lo[:, t, f * P:(f + 1) * P], moving[:, kt, 0],
                                      start=False, stop=(kt == KT - 1), skip_group_check=True)
                m.then_inc(piece_used, 1)

            def rows_are_tokens(n, stationary, halves=range(TH)):
                hi, lo = halves_of(n)
                g, a = divmod(n, PPG)
                for t in range(TPP):
                    kt = a * TPP + t
                    for h in halves:
                        acc = ps[:, bank0(g) + h, :]
                        tok = slice(h * P, (h + 1) * P)
                        pe.matmul(acc, stationary[:, kt, 0, tok], hi[:, t, :], start=(kt == 0), stop=False)
                        pe.matmul(acc, stationary[:, kt, 0, tok], lo[:, t, :], start=False, stop=False)
                        m = pe.matmul(acc, stationary[:, kt, 1, tok], hi[:, t, :], start=False, stop=(kt == KT - 1))
                return m

            def scores(g, pair):
                for f in range(2 * pair, 2 * pair + 2):
                    b = bank0(g + 1) + f
                    if g == MEM_JOB:
                        pe.wait_ge(mk_scaled, 1)
                        for h in range(TH):
                            m = pe.matmul(ps[:, b, h * M:(h + 1) * M], qmT[:, f, h * P:(h + 1) * P], mkT[:, f, :],
                                          start=True, stop=True)
                    else:
                        head = NF * CAUSAL_JOBS[g] + f
                        pe.matmul(ps[:, b, 0:P], qT[:, head, 0:P], kT[:, head, 0:P], start=True, stop=True)
                        m = pe.matmul(ps[:, b, P:P + S], qT[:, head, P:S], kT[:, head, :], start=True, stop=True)
                m.then_inc(scores_ready, 1)

            def turn_probs(g, pair):
                pe.wait_ge(probs_ready, 2 * JOBS.index(g) + pair + 1)
                for f in range(2 * pair, 2 * pair + 2):
                    b = bank0(g + 1) + f
                    if g == MEM_JOB:
                        for h in range(TH):
                            for k in range(TH):
                                m = pe.transpose(ps[:, b, k * S + h * P:k * S + (h + 1) * P],
                                                 probs_end[:, f, h * M + k * P:h * M + (k + 1) * P], ident[:, :])
                    else:
                        for c in range(3):
                            m = pe.transpose(ps[:, b, c * P:(c + 1) * P], probs[:, f, c * P:(c + 1) * P], ident[:, :])
                m.then_inc(probs_turned, 1)

            def weigh_values(g, pair):
                pe.wait_ge(probsT_ready, 2 * JOBS.index(g) + pair + 1)
                for f in range(2 * pair, 2 * pair + 2):
                    b = bank0(g + 1) + f
                    if g == MEM_JOB:
                        for k in range(TH):
                            m = pe.matmul(ps[:, b, 0:S], mv[:, k, f * HD:(f + 1) * HD],
                                          probs_end[:, NF + f, k * S:(k + 1) * S], start=(k == 0), stop=(k == 1))
                    else:
                        c = (NF * CAUSAL_JOBS[g] + f) * HD
                        pe.matmul(ps[:, b, 0:S], v[:, 0, c:c + HD], probsT[:, f, 0:S], start=True, stop=False)
                        m = pe.matmul(ps[:, b, P:S], v[:, 1, c:c + HD], probsT[:, f, S:S + P],
                                      start=False, stop=True)
                m.then_inc(pv_done, 1)

            pe.wait_ge(ones_ready, 1)
            for i in range(WARM_UP):
                pe.matmul(ps[:, 1, 0:P], ones[:, :], ones[:, :], start=True, stop=True)
            pe.wait_ge(rows_landed, 48)
            pe.wait_ge(consts_ready, 3)
            pe.transpose(ps[:, 0, 0:2 * KT + NF], rows[:, :], ident[0:2 * KT + NF, 0:2 * KT + NF]).then_inc(rows_turned, 1)
            for b in range(MEM_BLOCKS // 2):
                pe.wait_ge(mem_landed[b], 16)
                turn_input(mem_nat, 0, range(4 * b, 4 * b + 4), 4)

            for n in range(PIECES):
                g, a = divmod(n, PPG)
                if a == 0 and 2 <= g < OUT0 + 2:
                    pe.wait_ge(evacuated, g - 1)
                if a == 0 and g >= OUT0 + 2:
                    pe.wait_ge(summed, g - 1 - OUT0)
                if a == 0 and g - 1 in BRANCHES:
                    pe.wait_ge(att_ready, 2 * (BRANCHES.index(g - 1) + 1))
                if a == 0 and g == Q1:
                    pe.wait_ge(spread_read, 1)
                if a == 0 and g == Q0:
                    pe.wait_ge(turned_lo, KT)
                if g == MK:
                    pe.wait_ge(turned_lo, a + 1)
                if g == MK and a == 0:
                    pe.wait_ge(cols_ready, 1)
                if g == MV and a == 0:
                    pe.wait_ge(turned_lo, KT // 2)
                if g >= OUT0 and a % 2 == 0:
                    pe.wait_ge(y_lo, min(a // 2 + 1, len(GATES)))
                pe.wait_ge(lo_done, n + 1)
                if g == LAST:
                    m = rows_are_tokens(n, yT, range(0, 1))
                    if a == PPG - 1:
                        m.then_inc(half_used, 1)
                elif g >= OUT0:
                    rows_are_tokens(n, yT).then_inc(piece_used, 1)
                elif g in TOKENS_ON_ROWS:
                    rows_are_tokens(n, memT if g == MV else xT).then_inc(piece_used, 1)
                else:
                    rows_are_features(n, memT if g == MK else xT)

                if g == MK and a in (1, 2):
                    pe.wait_ge(mem_landed[a + 1], 16)
                    pe.wait_ge(turned_lo, 2 * a)
                    turn_input(mem_nat, 0, range(4 * a + 4, 4 * a + 8), 4)
                if g == MV and a == 1:
                    pe.wait_ge(turned_lo, KT // 2)
                    pe.wait_ge(diag_ready, 1)
                    for h in range(TH):
                        m = pe.matmul(ps[:, 7, h * P:(h + 1) * P], ones[:, :], diag[:, h], start=True, stop=True)
                    m.then_inc(spread, 1)
                if g == MV and a in (3, 5):
                    if a == 3:
                        pe.wait_ge(evacuated, MK + 1)
                        pe.wait_ge(scaled, 2)
                    else:
                        pe.wait_ge(turned_lo, KT // 2 + 4)
                    turn_input(x_nat, 1, range(4 * (a - 3), 4 * (a - 3) + 8), 0)
                if g in JOBS:
                    if a == 0:
                        pe.wait_ge(evacuated, g)
                        scores(g, 0)
                        scores(g, 1)
                    if a == 4:
                        turn_probs(g, 0)
                    if a == 5:
                        turn_probs(g, 1)
                        weigh_values(g, 0)
                    if a == 6:
                        weigh_values(g, 1)
                if g == GP and a == 5:
                    pe.wait_ge(wp_landed, 16)
                    pe.wait_ge(pooled_ready, NF)
                    for i in range(NF):
                        m = pe.matmul(ps[:, bank0(g + 1) + i, 0:S], wp[:, i, :], u_pad[:, i, PAD:], start=True, stop=True)
                    m.then_inc(mixed, 1)
            for a in range(PPG):
                m = rows_are_tokens(LAST * PPG + a, yT, range(1, 2))
            m.then_inc(half_used, 1)

        @block.scalar
        def _(act):
            def split_hi(n):
                act.wait_ge(landed[n % RAW], 16 * (n // RAW + 1))
                if SPLIT <= n < LAST * PPG:
                    act.wait_ge(piece_used, n - SPLIT + 1)
                elif n == LAST * PPG:
                    act.wait_ge(piece_used, OUT0 * PPG)
                elif n >= LAST * PPG + SPLIT:
                    act.wait_ge(piece_used, n - 2 * SPLIT + 1)
                act.activation(halves_of(n)[0], w_raw[:, n % RAW], ACT.Copy).then_inc(hi_done, 1)

            def square_input(nat, i, h):
                if 2 * i + h:
                    act.wait_ge(squared, 2 * i + h)
                act.activation(squares[:, :], nat[:, h, :], ACT.Square,
                               accum_out=ssq_in[:, i, h:h + 1]).then_inc(squared, 1)

            def turned_to_hi(dst, i, b, bank):
                act.wait_ge(turned, KT // 2 * i + b + 1)
                for kt in (2 * b, 2 * b + 1):
                    gain = (KT if i == 0 else 0) + kt
                    m = act.activation(dst[:, kt, 0], ps[:, bank + b % 4, kt % 2 * S:(kt % 2 + 1) * S], ACT.Copy,
                                       scale=cols[:, gain:gain + 1])
                m.then_inc(turned_hi, 1)

            def exps(g, pair):
                j = 2 * JOBS.index(g) + pair
                act.wait_ge(max_ready, j + 1)
                for f in range(2 * pair, 2 * pair + 2):
                    for h in range(TH):
                        c, w = (h * M, M) if g == MEM_JOB else (h * P, P + h * P)
                        dst = probs_end if g == MEM_JOB else probs
                        m = act.activation(dst[:, f, c:c + w], ps[:, bank0(g + 1) + f, c:c + w], ACT.Exp,
                                           bias=nmax[:, f, h:h + 1], accum_out=sums[:, f, h:h + 1])
                m.then_inc(exp_done, 1)

            def copy_probsT(g, pair):
                j = 2 * JOBS.index(g) + pair
                act.wait_ge(probs_turned, j + 1)
                if j == 0:
                    act.wait_ge(mk_scaled, 1)
                w = 2 * S if g == MEM_JOB else S + P
                b = bank0(g + 1) + 2 * pair
                dst = probs_end[:, NF + 2 * pair:NF + 2 * pair + 2] if g == MEM_JOB else probsT[:, 2 * pair:2 * pair + 2]
                act.activation(dst[:, :, 0:w], ps[:, b:b + 2, 0:w], ACT.Copy).then_inc(probsT_ready, 1)

            def copy_att(g, pair):
                j = JOBS.index(g)
                act.wait_ge(pv_done, 2 * j + pair + 1)
                if g == MEM_JOB:
                    act.wait_ge(y_ready, 2)
                b = bank0(g + 1) + 2 * pair
                act.activation(att[:, min(j, 1), 2 * pair:2 * pair + 2], ps[:, b:b + 2, 0:S],
                               ACT.Copy).then_inc(att_ready, 1)

            act.dma_start(rows[KT:2 * KT, :], mem_norm_g.rearrange("a (r c) -> (a r) c", c=P)).then_inc(rows_landed, 16)
            act.dma_start(rows[0:KT, :], norm_g.rearrange("a (r c) -> (a r) c", c=P)).then_inc(rows_landed, 16)
            act.dma_start(rows[2 * KT:, :], pool_scale.rearrange("a (r c) -> (a r) c", c=P)).then_inc(rows_landed, 16)
            act.wait_ge(ones_ready, 1)
            act.activation(nmax[:, 0, 0:1], ones[:, 0:1], ACT.Exp).then_inc(table_loaded, 1)

            act.wait_ge(cols_ready, 1)
            for b in range(KT // 4):
                turned_to_hi(memT, 0, b, 4)
                split_hi(b)

            for n in range(PIECES):
                g, a = divmod(n, PPG)
                if a == PPG - 1 and g < OUT0 and g not in TOKENS_ON_ROWS:
                    act.wait_ge(piece_used, n + 1)
                    if g >= 1:
                        act.wait_ge(evacuated, g)
                    if g - 1 in GATES:
                        act.wait_ge(y_ready, GATES.index(g - 1) + 1)
                    act.activation(part_b[:, :, :], ps[:, bank0(g):bank0(g) + NF, S:2 * S], ACT.Copy,
                                   scale=FACTOR.get(g, 1.0)).then_inc(part_b_ready, 1)
                if g == MK and a in (1, 2):
                    turned_to_hi(memT, 0, 2 * a + 2, 4)
                    turned_to_hi(memT, 0, 2 * a + 3, 4)
                for m in pieces_to_split(n):
                    split_hi(m)
                if g == MK and a in (0, 3):
                    if a == 0:
                        for b in range(MEM_BLOCKS):
                            act.wait_ge(mem_landed[b], 16)
                    square_input(mem_nat, 0, a // 3)
                if g == MK and a in (4, 5):
                    act.wait_ge(x_landed[a - 4], 16)
                    square_input(x_nat, 1, a - 4)
                if g == MV and a in (3, 5):
                    for b in range(2 * (a - 3), 2 * (a - 3) + 4):
                        turned_to_hi(xT, 1, b, 0)
                if g in JOBS:
                    if a == 0:
                        exps(g, 0)
                        exps(g, 1)
                    if a == 4:
                        copy_probsT(g, 0)
                    if a == 5:
                        copy_probsT(g, 1)
                        copy_att(g, 0)
                    if a == 6:
                        copy_att(g, 1)
                if g == GA1 and a == 2:
                    act.wait_ge(scores_ready, 4)
                    for h in range(TH):
                        act.dma_start(x_res[:, h], x_dram[h]).then_inc(res_landed, 16)
                    act.dma_start(fg[:, :], final_g.rearrange("(a d) -> a d", a=1).partition_broadcast(P)
                                  ).then_inc(fg_landed, 16)
                if g == GP and a == 5:
                    act.wait_ge(mixed, 1)
                    act.wait_ge(y_ready, 1)
                    for i in range(NF):
                        m = act.activation(att[:, 0, i], ps[:, bank0(g + 1) + i, 0:S], ACT.Copy,
                                           scale=cols[:, 2 * KT + i:2 * KT + i + 1])
                        if i % 2:
                            m.then_inc(att_ready, 1)
                if g in GATES and a == PPG - 1:
                    act.wait_ge(evacuated, g + 1)
                    act.activation(part_b[:, :, :], gate[:, :, :], ACT.Tanh).then_inc(gate_tanh, 1)
                if g - 1 in GATES:
                    i = GATES.index(g - 1)
                    if a == 1:
                        act.wait_ge(y_ready, i + 1)
                        act.activation(yT[:, NF * i:NF * (i + 1), 0], gate[:, :, :], ACT.Copy).then_inc(y_hi, 1)
                if OUT0 <= g < LAST and a == PPG - 1:
                    c = (g - OUT0) * COLS
                    act.wait_ge(summed, g - OUT0 + 1)
                    for h in range(TH):
                        act.wait_ge(sq_done, TH * (g - OUT0) + h) if g > OUT0 or h else None
                        act.activation(squares[:, 0:COLS], x_res[:, h, c:c + COLS], ACT.Square,
                                       accum_out=ssq[:, h, g - OUT0:g - OUT0 + 1]).then_inc(sq_done, 1)
            for h in range(TH):
                act.wait_ge(summed, LAST - OUT0 + h + 1)
                act.wait_ge(sq_done, TH * (LAST - OUT0) + h)
                act.activation(squares[:, 0:COLS], x_res[:, h, D - COLS:], ACT.Square,
                               accum_out=ssq[:, h, LAST - OUT0:]).then_inc(sq_done, 1)
                act.wait_ge(rstd2_ready, h + 1)
                act.activation(end_scaled[:, h], end_scaled[:, h], ACT.Copy, scale=rstd[:, h:h + 1]).then_inc(finished_act, 1)

        @block.vector
        def _(dve):
            steps = [0]

            def settle(ins):
                steps[0] += 1
                ins.then_inc(dve_self, 1)
                dve.wait_ge(dve_self, steps[0])

            def split_lo(n):
                hi, lo = halves_of(n)
                dve.wait_ge(hi_done, n + 1)
                dve.tensor_tensor(lo, w_raw[:, n % RAW], hi.bitcast(F32), ALU.subtract).then_inc(lo_done, 1)

            def mean_square(i):
                dve.wait_ge(squared, 2 * i + 2)
                dve.tensor_scalar(ms_in[:, i], ssq_in[:, i], 1.0 / D, EPS, ALU.mult, ALU.add).then_inc(ms_ready, 1)

            def turned_to_lo(dst, i, b, bank):
                dve.wait_ge(turned_hi, KT // 2 * i + b + 1)
                for kt in (2 * b, 2 * b + 1):
                    gain = (KT if i == 0 else 0) + kt
                    m = dve.scalar_tensor_tensor(out=dst[:, kt, 1], in0=ps[:, bank + b % 4, kt % 2 * S:(kt % 2 + 1) * S],
                                                 scalar=cols[:, gain:gain + 1], in1=dst[:, kt, 0].bitcast(F32),
                                                 op0=ALU.mult, op1=ALU.subtract)
                m.then_inc(turned_lo, 1)

            def evacuate(g):
                if g == MV:
                    for h in range(TH):
                        m = dve.tensor_scalar(mv[:, h], ps[:, bank0(g) + h, :], rstd_in[:, 0, h:h + 1], None, ALU.mult)
                    m.then_inc(evacuated, 1)
                    return
                if g in TOKENS_ON_ROWS:
                    dst = {V0: v[:, :, 0:COLS], V1: v[:, :, COLS:]}[g]
                    dve.tensor_copy(dst, ps[:, bank0(g):bank0(g) + TH, :]).then_inc(evacuated, 1)
                    return
                dst = {MK: mkT, QM: qmT, Q0: qT[:, 0:NF], Q1: qT[:, NF:], K0: kT[:, 0:NF], K1: kT[:, NF:],
                       U: u_pad[:, :, PAD:]}.get(g, gate)
                dve.wait_ge(part_b_ready, sum(i not in TOKENS_ON_ROWS for i in range(g + 1)))
                if g in GATES and g != GA0:
                    dve.wait_ge(y_lo, GATES.index(g))
                hi_part = ps[:, bank0(g):bank0(g) + NF, 0:S]
                dve.scalar_tensor_tensor(out=dst[:, :, :], in0=hi_part, scalar=FACTOR.get(g, 1.0), in1=part_b[:, :, :],
                                         op0=ALU.mult, op1=ALU.add).then_inc(evacuated, 1)

            def mask_and_max(g, pair):
                j = 2 * JOBS.index(g) + pair
                dve.wait_ge(scores_ready, j + 1)
                b = bank0(g + 1) + 2 * pair
                own = slice(2 * pair, 2 * pair + 2)
                if g == MEM_JOB:
                    dve.tensor_reduce(nmax[:, own, :], ps[:, b:b + 2, :].rearrange("p f (h k) -> p f h k", h=TH),
                                      AX.X, ALU.max, negate=True).then_inc(max_ready, 1)
                    return
                diag = ps[:, b:b + 2, :].rearrange("p f (h k) -> p f h k", h=TH)[:, :, :, 0:P]
                settle(dve.tensor_tensor(diag, diag, mask[:, :].rearrange("p (f h k) -> p f h k", f=1, h=1)
                                         .to_broadcast([P, 2, TH, P]), ALU.add))
                dve.tensor_reduce(nmax[:, own, 0:1], ps[:, b:b + 2, 0:P], AX.X, ALU.max, negate=True)
                dve.tensor_reduce(nmax[:, own, 1:2], ps[:, b:b + 2, P:P + S], AX.X, ALU.max,
                                  negate=True).then_inc(max_ready, 1)

            def normalise(g, pair):
                j = 2 * JOBS.index(g) + pair
                dve.wait_ge(exp_done, j + 1)
                own = slice(2 * pair, 2 * pair + 2)
                settle(dve.reciprocal(rsum[:, own, :], sums[:, own, :]))
                for h in range(TH):
                    c, w = (h * M, M) if g == MEM_JOB else (h * P, P + h * P)
                    part = (probs_end if g == MEM_JOB else probs)[:, own, c:c + w]
                    m = dve.tensor_tensor(part, part, rsum[:, own, h:h + 1].to_broadcast([P, 2, w]), ALU.mult)
                m.then_inc(probs_ready, 1)

            def pool_windows():
                dve.wait_ge(evacuated, U + 1)
                dve.wait_ge(pads_zero, 3)
                dve.wait_ge(consts_ready, 3 + NF)
                src = u_pad
                for i in range(NF):
                    dst, sh = (sum_a, sum_b)[i % 2], 1 << i
                    settle(dve.tensor_tensor(dst[:, i:, PAD:], src[:, i:, PAD:], src[:, i:, PAD - sh:PAD - sh + S],
                                             ALU.add))
                    src = dst
                for i, w in enumerate(WINDOWS):
                    total = (sum_a, sum_b)[i % 2]
                    first = slice(PAD, PAD + WINDOWS[-1])
                    rest = slice(PAD + WINDOWS[-1], PAD + S)
                    settle(dve.tensor_tensor(total[:, i, first], total[:, i, first], inv_cnt[:, i, :], ALU.mult))
                    settle(dve.tensor_tensor(u_pad[:, i, first], total[:, i, first], u_pad[:, i, first], ALU.subtract))
                    dve.scalar_tensor_tensor(out=u_pad[:, i, rest], in0=total[:, i, rest], scalar=1.0 / w,
                                             in1=u_pad[:, i, rest], op0=ALU.mult, op1=ALU.subtract
                                             ).then_inc(pooled_ready, 1)

            dve.wait_ge(table_loaded, 1)
            dve.wait_ge(rows_turned, 1)
            dve.tensor_copy(cols[:, :], ps[:, 0, 0:2 * KT + NF]).then_inc(cols_ready, 1)
            for b in range(KT // 4):
                turned_to_lo(memT, 0, b, 4)
                split_lo(b)

            for n in range(PIECES):
                g, a = divmod(n, PPG)
                if a == PPG - 1 and g < OUT0:
                    dve.wait_ge(piece_used, n + 1)
                    evacuate(g)
                if g == MK and a in (1, 2):
                    turned_to_lo(memT, 0, 2 * a + 2, 4)
                    turned_to_lo(memT, 0, 2 * a + 3, 4)
                for m in pieces_to_split(n):
                    split_lo(m)
                if g == MK and a == 4:
                    mean_square(0)
                if g == MK and a == 5:
                    dve.wait_ge(rstd_ready, 1)
                    for h in range(TH):
                        m = dve.tensor_scalar(diag[:, h], ident[:, :], rstd_in[:, 0, h:h + 1], None, ALU.mult)
                    m.then_inc(diag_ready, 1)
                if g == MK and a == 6:
                    mean_square(1)
                if g == MV and a == 1:
                    dve.wait_ge(spread, 1)
                    dve.tensor_copy(mem_rstd[:, 0, :], ps[:, 7, 0:M]).then_inc(spread_read, 1)
                if g == MV and a == 0:
                    dve.wait_ge(rstd_ready, 2)
                    for h in range(TH):
                        dve.tensor_scalar(x_nat[:, h, :], x_nat[:, h, :], rstd_in[:, 1, h:h + 1], None,
                                          ALU.mult).then_inc(scaled, 1)
                if g == MV and a in (3, 5):
                    for b in range(2 * (a - 3), 2 * (a - 3) + 4):
                        turned_to_lo(xT, 1, b, 0)
                if g in JOBS:
                    if a == 0:
                        mask_and_max(g, 0)
                        mask_and_max(g, 1)
                    if a == 1:
                        normalise(g, 0)
                    if a == 2:
                        normalise(g, 1)
                if g == GP and a == 0:
                    pool_windows()
                if g - 1 in GATES:
                    i = GATES.index(g - 1)
                    if a == 1:
                        dve.wait_ge(gate_att, i + 1)
                        dve.scalar_tensor_tensor(out=gate[:, :, :], in0=part_b[:, :, :], scalar=1.0, in1=gate[:, :, :],
                                                 op0=ALU.add, op1=ALU.mult).then_inc(y_ready, 1)
                    if a == 2:
                        dve.wait_ge(y_hi, i + 1)
                        own = slice(NF * i, NF * (i + 1))
                        dve.tensor_tensor(yT[:, own, 1], gate[:, :, :], yT[:, own, 0].bitcast(F32),
                                          ALU.subtract).then_inc(y_lo, 1)
                if OUT0 <= g < LAST and a == PPG - 1:
                    dve.wait_ge(piece_used, n + 1)
                    if g == OUT0:
                        dve.wait_ge(res_landed, 16 * TH)
                    c = (g - OUT0) * COLS
                    dve.tensor_tensor(x_res[:, :, c:c + COLS], ps[:, bank0(g):bank0(g) + TH, :],
                                      x_res[:, :, c:c + COLS], ALU.add).then_inc(summed, 1)
            dve.wait_ge(sq_done, TH * (LAST - OUT0))
            settle(dve.tensor_reduce(sst[:, :], ssq[:, :, 0:LAST - OUT0], AX.X, ALU.add))
            settle(dve.tensor_scalar(sst[:, :], sst[:, :], 1.0 / D, EPS, ALU.mult, ALU.add))
            for h in range(TH):
                dve.wait_ge(half_used, h + 1)
                dve.tensor_tensor(x_res[:, h, D - COLS:], ps[:, bank0(LAST) + h, :], x_res[:, h, D - COLS:],
                                  ALU.add).then_inc(summed, 1)
                dve.wait_ge(summed, LAST - OUT0 + h + 1)
                dve.wait_ge(fg_landed, 16)
                dve.tensor_tensor(end_scaled[:, h], x_res[:, h, D - COLS:], fg[:, D - COLS:], ALU.mult)
                dve.wait_ge(sq_done, TH * (LAST - OUT0) + h + 1)
                dve.tensor_scalar(ms[:, h:h + 1], ssq[:, h, LAST - OUT0:], 1.0 / D, sst[:, h:h + 1], ALU.mult,
                                  ALU.add).then_inc(ms2_ready, 1)
                dve.wait_ge(rstd2_ready, h + 1)
                dve.wait_ge(weighted, TH * (LAST - OUT0))
                for c in range(0, D - COLS, COLS):
                    dve.tensor_scalar(x_res[:, h, c:c + COLS], x_res[:, h, c:c + COLS], rstd[:, h:h + 1], None,
                                      ALU.mult).then_inc(finished_dve, 1)


_INS = ["x", "mem", "norm_g", "mem_norm_g", "w_in", "w_mem_kv", "w_pool", "pool_scale", "w_out", "final_norm_g"]


def kernel(**inputs):
    import numpy as _np
    import concourse.bacc as _bacc
    from concourse import mybir as _mybir
    from concourse.bass_utils import run_bass_kernel_spmd as _run

    nc = _bacc.Bacc("TRN2", target_bir_lowering=False, num_devices=1)
    arrays, args = {}, []
    for name in _INS:
        a = _np.ascontiguousarray(inputs[name])
        arrays[f"in_{name}"] = a
        args.append(nc.dram_tensor(f"in_{name}", a.shape, _mybir.dt.from_np(a.dtype), kind="ExternalInput").ap())
    args.append(nc.dram_tensor("out_0", (1, S, D), F32, kind="ExternalOutput").ap())
    build(nc, *args)
    r = _run(nc, [arrays], core_ids=[0])
    return r.results[0]["out_0"]
```

```python
from contextlib import ExitStack

import concourse.bass as bass
from concourse import mybir

F32 = mybir.dt.float32
F32R = mybir.dt.float32r
ALU = mybir.AluOpType
ACT = mybir.ActivationFunctionType
AX = mybir.AxisListType

P = 128
D = 2048
S = 256
M = 256
HD = 128
KT = D // P
COLS = 512
NF = COLS // P
TH = S // P
EPS = 1e-6
SCALE = HD ** -0.5
WINDOWS = (2, 4, 8, 16)
PAD = WINDOWS[-1] // 2
MASKED = -3.0e38

TPP = 2
PPG = KT // TPP
MC = TPP * P
RAW = 8
SPLIT = 4

(MK, MV, Q0, Q1, K0, K1, V0, V1, GA0, GA1, U, GP, QM, GM, OUT0) = range(15)
GROUPS = OUT0 + D // COLS
LAST = GROUPS - 1
PIECES = GROUPS * PPG
TOKENS_ON_ROWS = (MV, V0, V1)
CAUSAL_JOBS = {V1: 0, GA0: 1}
MEM_JOB = GM
JOBS = (V1, GA0, GM)
FACTOR = {Q0: SCALE, Q1: SCALE, QM: SCALE, GA0: 0.5, GA1: 0.5, GP: 0.5, GM: 0.5}
BRANCHES = (V1, GA0, GP, GM)
SQUARE_STEPS = {1: (0,), 2: (1,), 3: (2,), 4: (3,), 6: (4, 5), 7: (6,), 8: (7,)}
GATES = (GA0, GA1, GP, GM)


def build(nc, x, mem, norm_g, mem_norm_g, w_in, w_mem_kv, w_pool, pool_scale, w_out, final_g, out):
    with ExitStack() as ctx:
        def sb(name, shape, dt=F32, stack=ctx):
            return stack.enter_context(nc.sbuf_tensor(name, shape, dt))

        def sem(name):
            return ctx.enter_context(nc.semaphore(name))

        w_raw = sb("w_raw", [P, RAW, TPP, COLS])
        w_hi = sb("w_hi", [P, SPLIT, TPP, COLS], F32R)
        w_lo = sb("w_lo", [P, SPLIT, TPP, COLS], F32R)
        early = ExitStack()
        xT = sb("xT", [P, KT, 2, S], F32R, early)
        early.close()
        w_end = sb("w_end", [P, SPLIT, 2, TPP, COLS], F32R)
        early = ExitStack()
        mem_nat = sb("mem_nat", [P, TH, D], F32, early)
        x_nat = sb("x_nat", [P, TH, D], F32, early)
        early.close()
        yT = sb("yT", [P, KT, 2, S], F32R)
        early = ExitStack()
        memT = sb("memT", [P, KT, 2, S], F32R, early)
        early.close()
        early = ExitStack()
        qT = sb("qT", [P, 2 * NF, S], F32, early)
        kT = sb("kT", [P, 2 * NF, S], F32, early)
        early.close()
        x_res = sb("x_res", [P, TH, D])
        early = ExitStack()
        qmT = sb("qmT", [P, NF, S], F32, early)
        early.close()
        v = sb("v", [P, TH, 2 * COLS])
        fg = sb("fg", [P, D])
        mkT = sb("mkT", [P, NF, S])
        mv = sb("mv", [P, TH, COLS])
        early = ExitStack()
        probs = sb("probs", [P, NF, 2 * S], F32, early)
        probsT = sb("probsT", [P, NF, 2 * S], F32, early)
        early.close()
        early = ExitStack()
        u_pad = sb("u_pad", [P, NF, PAD + S], F32, early)
        sum_a = sb("sum_a", [P, NF, PAD + S], F32, early)
        sum_b = sb("sum_b", [P, NF, PAD + S], F32, early)
        early.close()
        early = ExitStack()
        squares = sb("squares", [P, D // 2], F32, early)
        kept = ExitStack()
        diag = sb("diag", [P, TH, P], F32, kept)
        mem_rstd = sb("mem_rstd", [P, 1, M], F32, kept)
        kept.close()
        end_scaled = sb("end_scaled", [P, TH, COLS], F32, early)
        early.close()
        probs_end = sb("probs_end", [P, 2 * NF, 2 * S])
        att = sb("att", [P, 2, NF, S])
        part_b = sb("part_b", [P, NF, S])
        gate = sb("gate", [P, NF, S])
        ident = sb("ident", [P, P])
        mask = sb("mask", [P, P])
        ones = sb("ones", [P, P])
        mem_rows = sb("mem_rows", [KT, P])
        x_rows = sb("x_rows", [KT + NF, P])
        mem_cols = sb("mem_cols", [P, KT])
        x_cols = sb("x_cols", [P, KT + NF])
        wp = sb("wp", [P, NF, P])
        inv_cnt = sb("inv_cnt", [P, NF, WINDOWS[-1]])
        nmax = sb("nmax", [P, NF, 2])
        sums = sb("sums", [P, NF, 2])
        rsum = sb("rsum", [P, NF, 2])
        ssq_in = sb("ssq_in", [P, 2, TH, 2])
        ms_in = sb("ms_in", [P, 2, TH])
        rstd_in = sb("rstd_in", [P, 2, TH])
        ssq = sb("ssq", [P, TH, D // COLS])
        sst = sb("sst", [P, TH])
        ms = sb("ms", [P, TH])
        rstd = sb("rstd", [P, TH])
        power = sb("power", [P, 2])

        ps = ctx.enter_context(nc.psum_tensor("ps", [P, 8, 512], F32))

        landed = [sem(f"landed{i}") for i in range(RAW)]
        first_landed = sem("first_landed")
        mem_rows_landed = sem("mem_rows_landed")
        x_rows_landed = sem("x_rows_landed")
        wp_landed = sem("wp_landed")
        mem_landed = [sem(f"mem_landed{i}") for i in range(PPG)]
        x_landed = [sem(f"x_landed{i}") for i in range(TH)]
        fg_landed = sem("fg_landed")
        res_landed = sem("res_landed")
        hi_done = sem("hi_done")
        lo_done = sem("lo_done")
        piece_used = sem("piece_used")
        consts_ready = sem("consts_ready")
        ones_ready = sem("ones_ready")
        pool_self = sem("pool_self")
        first_hi = sem("first_hi")
        first_lo = sem("first_lo")
        rows_turned = sem("rows_turned")
        cols_ready = sem("cols_ready")
        squared = sem("squared")
        ms_ready = sem("ms_ready")
        rstd_ready = sem("rstd_ready")
        table_loaded = sem("table_loaded")
        scaled = sem("scaled")
        diag_ready = sem("diag_ready")
        spread = sem("spread")
        spread_read = sem("spread_read")
        mk_scaled = sem("mk_scaled")
        turned = sem("turned")
        turned_hi = sem("turned_hi")
        turned_lo = sem("turned_lo")
        part_b_ready = sem("part_b_ready")
        evacuated = sem("evacuated")
        scores_ready = sem("scores_ready")
        max_ready = sem("max_ready")
        exp_done = sem("exp_done")
        probs_ready = sem("probs_ready")
        probs_turned = sem("probs_turned")
        probsT_ready = sem("probsT_ready")
        pv_done = sem("pv_done")
        att_ready = sem("att_ready")
        pads_zero = sem("pads_zero")
        pooled_ready = sem("pooled_ready")
        mixed = sem("mixed")
        gate_tanh = sem("gate_tanh")
        gate_att = sem("gate_att")
        y_ready = sem("y_ready")
        y_hi = sem("y_hi")
        y_lo = sem("y_lo")
        summed = sem("summed")
        sq_done = sem("sq_done")
        weighted = sem("weighted")
        half_used = sem("half_used")
        ms2_ready = sem("ms2_ready")
        rstd2_ready = sem("rstd2_ready")
        end_weighted = sem("end_weighted")
        finished_dve = sem("finished_dve")
        finished_act = sem("finished_act")
        stored = sem("stored")
        dve_self = sem("dve_self")

        end = slice(D - COLS, D)

        def pieces_of(w):
            return w.rearrange("(a t p) (g c) -> g a p t c", t=TPP, p=P, c=COLS)

        kv_dram, in_dram, out_w_dram = pieces_of(w_mem_kv[0]), pieces_of(w_in[0]), pieces_of(w_out[0])
        x_dram = x[0].rearrange("(h p) d -> h p d", p=P)
        out_dram = out[0].rearrange("(h p) d -> h p d", p=P)

        def bank0(g):
            return 4 * (g % 2)

        def halves_of(n):
            if LAST * PPG <= n < LAST * PPG + SPLIT:
                return w_end[:, n % SPLIT, 0], w_end[:, n % SPLIT, 1]
            return w_hi[:, n % SPLIT], w_lo[:, n % SPLIT]

        def pieces_to_split(n):
            ahead = n - (LAST * PPG - SPLIT)
            if ahead < 0:
                return range(n + SPLIT, n + SPLIT + 1)
            return range(min(n + SPLIT + ahead, PIECES), min(n + SPLIT + ahead + 2, PIECES))

        block = ctx.enter_context(nc.Block())

        @block.sync
        def _(sp):
            for a in range(PPG):
                c = slice(a * MC, (a + 1) * MC)
                sp.dma_start(mem_nat[:, :, c], mem[0, :, c].rearrange("(h p) d -> p h d", p=P)).then_inc(mem_landed[a], 16)
                if a == 0:
                    sp.dma_start(w_raw[:, 0, 0], kv_dram[0, 0, :, 0]).then_inc(first_landed, 16)
                    sp.dma_start(w_raw[:, 0, 1], kv_dram[0, 0, :, 1]).then_inc(landed[0], 16)
                else:
                    sp.dma_start(w_raw[:, a], kv_dram[0, a]).then_inc(landed[a], 16)
            for a in range(PPG):
                sp.wait_ge(lo_done, a + 1)
                sp.dma_start(w_raw[:, a], kv_dram[1, a]).then_inc(landed[a], 16)
                if a in (1, 2):
                    sp.dma_start(x_nat[:, a - 1], x_dram[a - 1]).then_inc(x_landed[a - 1], 16)
            sp.dma_start(wp[:, :, :], w_pool[0].rearrange("g c d -> c g d")).then_inc(wp_landed, 16)
            with sp.Fori(0, OUT0 - Q0) as g:
                for a in range(PPG):
                    sp.wait_ge(lo_done, g * PPG + (PPG + a + 1))
                    sp.dma_start(w_raw[:, a], in_dram[bass.ds(g, 1), a].rearrange("g p t c -> p (g t) c")
                                 ).then_inc(landed[a], 16)
            with sp.Fori(0, GROUPS - OUT0) as g:
                for a in range(PPG):
                    sp.wait_ge(lo_done, g * PPG + ((OUT0 - 1) * PPG + a + 1))
                    sp.dma_start(w_raw[:, a], out_w_dram[bass.ds(g, 1), a].rearrange("g p t c -> p (g t) c")
                                 ).then_inc(landed[a], 16)
            for h in range(TH):
                for i in range(3):
                    c = slice(i * COLS, (i + 1) * COLS)
                    sp.wait_ge(finished_dve, 3 * h + i + 1)
                    sp.dma_start(out_dram[h, :, c], x_res[:, h, c]).then_inc(stored, 16)
                sp.wait_ge(finished_act, h + 1)
                sp.dma_start(out_dram[h, :, D - COLS:], end_scaled[:, h]).then_inc(stored, 16)
            sp.wait_ge(stored, 16 * 4 * TH)

        @block.gpsimd
        def _(pool):
            pool.memset(ones[:, :], 1.0).then_inc(ones_ready, 1)
            pool.memset(ident[:, :], 0.0).then_inc(pool_self, 1)
            pool.memset(mask[:, :], 0.0).then_inc(pool_self, 1)
            pool.memset(power[:, :], -0.5).then_inc(consts_ready, 1)
            pool.wait_ge(pool_self, 2)
            pool.affine_select(out=ident[:, :], in_=ident[:, :], compare_op=ALU.not_equal, fill=1.0, base=0,
                               pattern=[[-1, P]], channel_multiplier=1).then_inc(consts_ready, 1)
            pool.affine_select(out=mask[:, :], in_=mask[:, :], compare_op=ALU.is_ge, fill=MASKED, base=0,
                               pattern=[[-1, P]], channel_multiplier=1).then_inc(consts_ready, 1)
            for t in range(WINDOWS[-1]):
                pool.memset(inv_cnt[:, :, t:t + 1], 1.0 / (t + 1)).then_inc(pool_self, 1)
            pool.wait_ge(pool_self, 2 + WINDOWS[-1])
            for i, w in enumerate(WINDOWS):
                pool.memset(inv_cnt[:, i, w - 1:], 1.0 / w).then_inc(consts_ready, 1)
            for i in range(2):
                pool.wait_ge(ms_ready, i + 1)
                pool.tensor_tensor(rstd_in[:, i], ms_in[:, i], power[:, :], ALU.pow).then_inc(rstd_ready, 1)
            pool.wait_ge(evacuated, MK + 1)
            pool.wait_ge(spread_read, 1)
            pool.tensor_tensor(mkT[:, :, :], mkT[:, :, :], mem_rstd[:, :, :].to_broadcast([P, NF, M]),
                               ALU.mult).then_inc(mk_scaled, 1)
            pool.wait_ge(pv_done, 4)
            for buf in (u_pad, sum_a, sum_b):
                pool.memset(buf[:, :, 0:PAD], 0.0).then_inc(pads_zero, 1)
            for i, g in enumerate(GATES):
                pool.wait_ge(gate_tanh, i + 1)
                pool.wait_ge(att_ready, 2 * (i + 1))
                pool.tensor_tensor(gate[:, :, :], gate[:, :, :], att[:, i % 2], ALU.mult).then_inc(gate_att, 1)
            pool.wait_ge(fg_landed, 16)
            for g in range(OUT0, LAST):
                c = (g - OUT0) * COLS
                pool.wait_ge(sq_done, TH * (g - OUT0 + 1))
                for h in range(TH):
                    pool.tensor_tensor(x_res[:, h, c:c + COLS], x_res[:, h, c:c + COLS], fg[:, c:c + COLS],
                                       ALU.mult).then_inc(weighted, 1)
            for h in range(TH):
                pool.wait_ge(ms2_ready, h + 1)
                pool.tensor_tensor(rstd[:, h:h + 1], ms[:, h:h + 1], power[:, 0:1], ALU.pow).then_inc(rstd2_ready, 1)

        @block.tensor
        def _(pe):
            def turn_input(nat, i, kts, bank):
                for kt in kts:
                    for h in range(TH):
                        c = kt % 2 * S + h * P
                        t = pe.transpose(ps[:, bank + kt // 2 % 4, c:c + P], nat[:, h, kt * P:(kt + 1) * P], ident[:, :])
                    if kt % 2:
                        t.then_inc(turned, 1)

            def rows_are_features(n, moving):
                hi, lo = halves_of(n)
                g, a = divmod(n, PPG)
                for t in range(TPP):
                    kt = a * TPP + t
                    if n == 0 and t == 1:
                        pe.wait_ge(lo_done, 1)
                    for f in range(NF):
                        acc = ps[:, bank0(g) + f, :]
                        pe.matmul(acc, hi[:, t, f * P:(f + 1) * P], moving[:, kt], start=(kt == 0),
                                  stop=(kt == KT - 1), skip_group_check=True)
                        m = pe.matmul(acc[:, 0:S], lo[:, t, f * P:(f + 1) * P], moving[:, kt, 0],
                                      start=False, stop=(kt == KT - 1), skip_group_check=True)
                m.then_inc(piece_used, 1)

            def rows_are_tokens(n, stationary, halves=range(TH)):
                hi, lo = halves_of(n)
                g, a = divmod(n, PPG)
                for t in range(TPP):
                    kt = a * TPP + t
                    for h in halves:
                        acc = ps[:, bank0(g) + h, :]
                        tok = slice(h * P, (h + 1) * P)
                        pe.matmul(acc, stationary[:, kt, 0, tok], hi[:, t, :], start=(kt == 0), stop=False)
                        pe.matmul(acc, stationary[:, kt, 0, tok], lo[:, t, :], start=False, stop=False)
                        m = pe.matmul(acc, stationary[:, kt, 1, tok], hi[:, t, :], start=False, stop=(kt == KT - 1))
                return m

            def scores(g, pair):
                for f in range(2 * pair, 2 * pair + 2):
                    b = bank0(g + 1) + f
                    if g == MEM_JOB:
                        pe.wait_ge(mk_scaled, 1)
                        for h in range(TH):
                            m = pe.matmul(ps[:, b, h * M:(h + 1) * M], qmT[:, f, h * P:(h + 1) * P], mkT[:, f, :],
                                          start=True, stop=True)
                    else:
                        head = NF * CAUSAL_JOBS[g] + f
                        pe.matmul(ps[:, b, 0:P], qT[:, head, 0:P], kT[:, head, 0:P], start=True, stop=True)
                        m = pe.matmul(ps[:, b, P:P + S], qT[:, head, P:S], kT[:, head, :], start=True, stop=True)
                m.then_inc(scores_ready, 1)

            def turn_probs(g, pair):
                pe.wait_ge(probs_ready, 2 * JOBS.index(g) + pair + 1)
                for f in range(2 * pair, 2 * pair + 2):
                    b = bank0(g + 1) + f
                    if g == MEM_JOB:
                        for h in range(TH):
                            for k in range(TH):
                                m = pe.transpose(ps[:, b, k * S + h * P:k * S + (h + 1) * P],
                                                 probs_end[:, f, h * M + k * P:h * M + (k + 1) * P], ident[:, :])
                    else:
                        for c in range(3):
                            m = pe.transpose(ps[:, b, c * P:(c + 1) * P], probs[:, f, c * P:(c + 1) * P], ident[:, :])
                m.then_inc(probs_turned, 1)

            def weigh_values(g, pair):
                pe.wait_ge(probsT_ready, 2 * JOBS.index(g) + pair + 1)
                for f in range(2 * pair, 2 * pair + 2):
                    b = bank0(g + 1) + f
                    if g == MEM_JOB:
                        for k in range(TH):
                            m = pe.matmul(ps[:, b, 0:S], mv[:, k, f * HD:(f + 1) * HD],
                                          probs_end[:, NF + f, k * S:(k + 1) * S], start=(k == 0), stop=(k == 1))
                    else:
                        c = (NF * CAUSAL_JOBS[g] + f) * HD
                        pe.matmul(ps[:, b, 0:S], v[:, 0, c:c + HD], probsT[:, f, 0:S], start=True, stop=False)
                        m = pe.matmul(ps[:, b, P:S], v[:, 1, c:c + HD], probsT[:, f, S:S + P],
                                      start=False, stop=True)
                m.then_inc(pv_done, 1)

            def keep_warm(count):
                for i in range(count):
                    pe.matmul(ps[:, 1, 0:P], ones[:, :], ones[:, :], start=True, stop=True)

            pe.wait_ge(ones_ready, 1)
            keep_warm(7)
            pe.wait_ge(mem_rows_landed, 16)
            pe.wait_ge(consts_ready, 3)
            pe.transpose(ps[:, 0, 0:KT], mem_rows[:, :], ident[0:KT, 0:KT]).then_inc(rows_turned, 1)
            for b in range(2):
                pe.wait_ge(mem_landed[b], 16)
                turn_input(mem_nat, 0, range(2 * b, 2 * b + 2), 4)
                keep_warm(4)

            for n in range(PIECES):
                g, a = divmod(n, PPG)
                if a == 0 and 2 <= g < OUT0 + 2:
                    pe.wait_ge(evacuated, g - 1)
                if a == 0 and g >= OUT0 + 2:
                    pe.wait_ge(summed, g - 1 - OUT0)
                if a == 0 and g - 1 in BRANCHES:
                    pe.wait_ge(att_ready, 2 * (BRANCHES.index(g - 1) + 1))
                if a == 0 and g == Q1:
                    pe.wait_ge(spread_read, 1)
                if a == 0 and g == Q0:
                    pe.wait_ge(turned_lo, KT)
                if g == MK:
                    pe.wait_ge(turned_lo, a + 1)
                if g == MK and a == 0:
                    pe.wait_ge(cols_ready, 1)
                if g == MV and a == 0:
                    pe.wait_ge(turned_lo, PPG)
                if g >= OUT0 and a % 2 == 0:
                    pe.wait_ge(y_lo, min(a // 2 + 1, len(GATES)))
                if n == 0:
                    pe.wait_ge(first_lo, 1)
                else:
                    pe.wait_ge(lo_done, n + 1)
                if g == LAST:
                    m = rows_are_tokens(n, yT, range(0, 1))
                    if a == PPG - 1:
                        m.then_inc(half_used, 1)
                elif g >= OUT0:
                    rows_are_tokens(n, yT).then_inc(piece_used, 1)
                elif g in TOKENS_ON_ROWS:
                    rows_are_tokens(n, memT if g == MV else xT).then_inc(piece_used, 1)
                else:
                    rows_are_features(n, memT if g == MK else xT)

                if g == MK and a + 2 < PPG:
                    pe.wait_ge(mem_landed[a + 2], 16)
                    if a >= 2:
                        pe.wait_ge(turned_lo, a - 1)
                    turn_input(mem_nat, 0, range(2 * a + 4, 2 * a + 6), 4)
                if g == MV and a == 1:
                    pe.wait_ge(turned_lo, PPG)
                    pe.wait_ge(x_rows_landed, 32)
                    pe.transpose(ps[:, 7, M:M + KT + NF], x_rows[:, :], ident[0:KT + NF, 0:KT + NF])
                    pe.wait_ge(diag_ready, 1)
                    for h in range(TH):
                        m = pe.matmul(ps[:, 7, h * P:(h + 1) * P], ones[:, :], diag[:, h], start=True, stop=True)
                    m.then_inc(spread, 1)
                if g == MV and a in (3, 5):
                    if a == 3:
                        pe.wait_ge(evacuated, MK + 1)
                        pe.wait_ge(scaled, 1)
                    else:
                        pe.wait_ge(scaled, 2)
                        pe.wait_ge(turned_lo, PPG + 4)
                    turn_input(x_nat, 1, range(4 * (a - 3), 4 * (a - 3) + 8), 0)
                if g in JOBS:
                    if a == 0:
                        pe.wait_ge(evacuated, g)
                        scores(g, 0)
                        scores(g, 1)
                    if a == 4:
                        turn_probs(g, 0)
                    if a == 5:
                        turn_probs(g, 1)
                        weigh_values(g, 0)
                    if a == 6:
                        weigh_values(g, 1)
                if g == GP and a == 5:
                    pe.wait_ge(wp_landed, 16)
                    pe.wait_ge(pooled_ready, NF)
                    for i in range(NF):
                        m = pe.matmul(ps[:, bank0(g + 1) + i, 0:S], wp[:, i, :], u_pad[:, i, PAD:], start=True, stop=True)
                    m.then_inc(mixed, 1)
            for a in range(PPG):
                m = rows_are_tokens(LAST * PPG + a, yT, range(1, 2))
            m.then_inc(half_used, 1)

        @block.scalar
        def _(act):
            def split_hi(n):
                if SPLIT <= n < LAST * PPG:
                    act.wait_ge(piece_used, n - SPLIT + 1)
                elif n == LAST * PPG:
                    act.wait_ge(piece_used, OUT0 * PPG)
                elif n >= LAST * PPG + SPLIT:
                    act.wait_ge(piece_used, n - 2 * SPLIT + 1)
                if n == 0:
                    act.wait_ge(first_landed, 16)
                    act.activation(w_hi[:, 0, 0], w_raw[:, 0, 0], ACT.Copy).then_inc(first_hi, 1)
                    act.wait_ge(landed[0], 16)
                    act.activation(w_hi[:, 0, 1], w_raw[:, 0, 1], ACT.Copy).then_inc(hi_done, 1)
                    return
                act.wait_ge(landed[n % RAW], 16 * (n // RAW + 1))
                act.activation(halves_of(n)[0], w_raw[:, n % RAW], ACT.Copy).then_inc(hi_done, 1)

            def square_input(k):
                if k < 4:
                    i, nat, c, h = 0, mem_nat, k // 2, k % 2
                    for b in range(PPG // 2 * c, PPG // 2 * (c + 1)):
                        act.wait_ge(mem_landed[b], 16)
                else:
                    i, nat, h, c = 1, x_nat, k // 2 - 2, k % 2
                    act.wait_ge(x_landed[h], 16)
                if k:
                    act.wait_ge(squared, k)
                act.activation(squares[:, 0:D // 2], nat[:, h, c * D // 2:(c + 1) * D // 2], ACT.Square,
                               accum_out=ssq_in[:, i, h, c:c + 1]).then_inc(squared, 1)

            def turned_to_hi(dst, i, b, bank):
                act.wait_ge(turned, KT // 2 * i + b + 1)
                gains = x_cols if i else mem_cols
                for kt in (2 * b, 2 * b + 1):
                    m = act.activation(dst[:, kt, 0], ps[:, bank + b % 4, kt % 2 * S:(kt % 2 + 1) * S], ACT.Copy,
                                       scale=gains[:, kt:kt + 1])
                m.then_inc(turned_hi, 1)

            def exps(g, pair):
                j = 2 * JOBS.index(g) + pair
                act.wait_ge(max_ready, j + 1)
                if j == 0:
                    act.wait_ge(mk_scaled, 1)
                for f in range(2 * pair, 2 * pair + 2):
                    for h in range(TH):
                        c, w = (h * M, M) if g == MEM_JOB else (h * P, P + h * P)
                        dst = probs_end if g == MEM_JOB else probs
                        m = act.activation(dst[:, f, c:c + w], ps[:, bank0(g + 1) + f, c:c + w], ACT.Exp,
                                           bias=nmax[:, f, h:h + 1], accum_out=sums[:, f, h:h + 1])
                m.then_inc(exp_done, 1)

            def copy_probsT(g, pair):
                j = 2 * JOBS.index(g) + pair
                act.wait_ge(probs_turned, j + 1)
                w = 2 * S if g == MEM_JOB else S + P
                b = bank0(g + 1) + 2 * pair
                dst = probs_end[:, NF + 2 * pair:NF + 2 * pair + 2] if g == MEM_JOB else probsT[:, 2 * pair:2 * pair + 2]
                act.activation(dst[:, :, 0:w], ps[:, b:b + 2, 0:w], ACT.Copy).then_inc(probsT_ready, 1)

            def copy_att(g, pair):
                j = JOBS.index(g)
                act.wait_ge(pv_done, 2 * j + pair + 1)
                if g == MEM_JOB:
                    act.wait_ge(y_ready, 2)
                b = bank0(g + 1) + 2 * pair
                act.activation(att[:, min(j, 1), 2 * pair:2 * pair + 2], ps[:, b:b + 2, 0:S],
                               ACT.Copy).then_inc(att_ready, 1)

            def square_sum(h, c, i):
                if sq_count[0]:
                    act.wait_ge(sq_done, sq_count[0])
                act.activation(squares[:, 0:c.stop - c.start], x_res[:, h, c], ACT.Square, scale=D ** -0.5,
                               accum_out=ssq[:, h, i:i + 1]).then_inc(sq_done, 1)
                sq_count[0] += 1

            sq_count = [0]
            act.dma_start(mem_rows[:, :], mem_norm_g.rearrange("a (r c) -> (a r) c", c=P)).then_inc(mem_rows_landed, 16)
            act.wait_ge(ones_ready, 1)
            act.activation(nmax[:, 0, 0:1], ones[:, 0:1], ACT.Exp).then_inc(table_loaded, 1)
            act.dma_start(x_rows[0:KT, :], norm_g.rearrange("a (r c) -> (a r) c", c=P)).then_inc(x_rows_landed, 16)
            act.dma_start(x_rows[KT:, :], pool_scale.rearrange("a (r c) -> (a r) c", c=P)).then_inc(x_rows_landed, 16)

            act.wait_ge(cols_ready, 1)
            for b in range(2):
                turned_to_hi(memT, 0, b, 4)
                split_hi(b)
            split_hi(2)

            for n in range(PIECES):
                g, a = divmod(n, PPG)
                if a == PPG - 1 and g < OUT0 and g not in TOKENS_ON_ROWS:
                    act.wait_ge(piece_used, n + 1)
                    if g >= 1:
                        act.wait_ge(evacuated, g)
                    if g - 1 in GATES:
                        act.wait_ge(y_ready, GATES.index(g - 1) + 1)
                    act.activation(part_b[:, :, :], ps[:, bank0(g):bank0(g) + NF, S:2 * S], ACT.Copy,
                                   scale=FACTOR.get(g, 1.0)).then_inc(part_b_ready, 1)
                if g == MK and a + 2 < PPG:
                    turned_to_hi(memT, 0, a + 2, 4)
                if n == 0:
                    split_hi(3)
                for m in pieces_to_split(n):
                    split_hi(m)
                for k in SQUARE_STEPS.get(n, ()):
                    square_input(k)
                if g == MV and a in (3, 5):
                    act.wait_ge(cols_ready, 2)
                    for b in range(2 * (a - 3), 2 * (a - 3) + 4):
                        turned_to_hi(xT, 1, b, 0)
                if g in JOBS:
                    if a == 0:
                        exps(g, 0)
                        exps(g, 1)
                    if a == 4:
                        copy_probsT(g, 0)
                    if a == 5:
                        copy_probsT(g, 1)
                        copy_att(g, 0)
                    if a == 6:
                        copy_att(g, 1)
                if g == GA1 and a == 2:
                    act.wait_ge(scores_ready, 4)
                    for h in range(TH):
                        act.dma_start(x_res[:, h], x_dram[h]).then_inc(res_landed, 16)
                    act.dma_start(fg[:, :], final_g.rearrange("(a d) -> a d", a=1).partition_broadcast(P)
                                  ).then_inc(fg_landed, 16)
                if g == GP and a == 5:
                    act.wait_ge(mixed, 1)
                    act.wait_ge(y_ready, 1)
                    for i in range(NF):
                        m = act.activation(att[:, 0, i], ps[:, bank0(g + 1) + i, 0:S], ACT.Copy,
                                           scale=x_cols[:, KT + i:KT + i + 1])
                        if i % 2:
                            m.then_inc(att_ready, 1)
                if g in GATES and a == PPG - 1:
                    act.wait_ge(evacuated, g + 1)
                    act.activation(part_b[:, :, :], gate[:, :, :], ACT.Tanh).then_inc(gate_tanh, 1)
                if g - 1 in GATES:
                    i = GATES.index(g - 1)
                    if a == 1:
                        act.wait_ge(y_ready, i + 1)
                        act.activation(yT[:, NF * i:NF * (i + 1), 0], gate[:, :, :], ACT.Copy).then_inc(y_hi, 1)
                if OUT0 <= g < LAST and a == PPG - 1:
                    c = (g - OUT0) * COLS
                    act.wait_ge(summed, g - OUT0 + 1)
                    for h in range(TH):
                        square_sum(h, slice(c, c + COLS), g - OUT0)
            for h in range(TH):
                act.wait_ge(summed, LAST - OUT0 + h + 1)
                square_sum(h, end, LAST - OUT0)
                act.wait_ge(end_weighted, h + 1)
                act.wait_ge(rstd2_ready, h + 1)
                act.activation(end_scaled[:, h], end_scaled[:, h], ACT.Copy, scale=rstd[:, h:h + 1]).then_inc(finished_act, 1)

        @block.vector
        def _(dve):
            steps = [0]

            def settle(ins):
                steps[0] += 1
                ins.then_inc(dve_self, 1)
                dve.wait_ge(dve_self, steps[0])

            def split_lo(n):
                hi, lo = halves_of(n)
                if n == 0:
                    dve.wait_ge(first_hi, 1)
                    dve.tensor_tensor(w_lo[:, 0, 0], w_raw[:, 0, 0], w_hi[:, 0, 0].bitcast(F32), ALU.subtract
                                      ).then_inc(first_lo, 1)
                    dve.wait_ge(hi_done, 1)
                    dve.tensor_tensor(w_lo[:, 0, 1], w_raw[:, 0, 1], w_hi[:, 0, 1].bitcast(F32), ALU.subtract
                                      ).then_inc(lo_done, 1)
                    return
                dve.wait_ge(hi_done, n + 1)
                dve.tensor_tensor(lo, w_raw[:, n % RAW], hi.bitcast(F32), ALU.subtract).then_inc(lo_done, 1)

            def mean_square(i):
                dve.wait_ge(squared, 4 * i + 4)
                settle(dve.tensor_reduce(ms_in[:, i], ssq_in[:, i], AX.X, ALU.add))
                dve.tensor_scalar(ms_in[:, i], ms_in[:, i], 1.0 / D, EPS, ALU.mult, ALU.add).then_inc(ms_ready, 1)

            def turned_to_lo(dst, i, b, bank):
                dve.wait_ge(turned_hi, KT // 2 * i + b + 1)
                gains = x_cols if i else mem_cols
                for kt in (2 * b, 2 * b + 1):
                    m = dve.scalar_tensor_tensor(out=dst[:, kt, 1], in0=ps[:, bank + b % 4, kt % 2 * S:(kt % 2 + 1) * S],
                                                 scalar=gains[:, kt:kt + 1], in1=dst[:, kt, 0].bitcast(F32),
                                                 op0=ALU.mult, op1=ALU.subtract)
                m.then_inc(turned_lo, 1)

            def evacuate(g):
                if g == MV:
                    for h in range(TH):
                        m = dve.tensor_scalar(mv[:, h], ps[:, bank0(g) + h, :], rstd_in[:, 0, h:h + 1], None, ALU.mult)
                    m.then_inc(evacuated, 1)
                    return
                if g in TOKENS_ON_ROWS:
                    dst = {V0: v[:, :, 0:COLS], V1: v[:, :, COLS:]}[g]
                    dve.tensor_copy(dst, ps[:, bank0(g):bank0(g) + TH, :]).then_inc(evacuated, 1)
                    return
                dst = {MK: mkT, QM: qmT, Q0: qT[:, 0:NF], Q1: qT[:, NF:], K0: kT[:, 0:NF], K1: kT[:, NF:],
                       U: u_pad[:, :, PAD:]}.get(g, gate)
                dve.wait_ge(part_b_ready, sum(i not in TOKENS_ON_ROWS for i in range(g + 1)))
                if g in GATES and g != GA0:
                    dve.wait_ge(y_lo, GATES.index(g))
                hi_part = ps[:, bank0(g):bank0(g) + NF, 0:S]
                dve.scalar_tensor_tensor(out=dst[:, :, :], in0=hi_part, scalar=FACTOR.get(g, 1.0), in1=part_b[:, :, :],
                                         op0=ALU.mult, op1=ALU.add).then_inc(evacuated, 1)

            def mask_and_max(g, pair):
                j = 2 * JOBS.index(g) + pair
                dve.wait_ge(scores_ready, j + 1)
                b = bank0(g + 1) + 2 * pair
                own = slice(2 * pair, 2 * pair + 2)
                if g == MEM_JOB:
                    dve.tensor_reduce(nmax[:, own, :], ps[:, b:b + 2, :].rearrange("p f (h k) -> p f h k", h=TH),
                                      AX.X, ALU.max, negate=True).then_inc(max_ready, 1)
                    return
                diag = ps[:, b:b + 2, :].rearrange("p f (h k) -> p f h k", h=TH)[:, :, :, 0:P]
                settle(dve.tensor_tensor(diag, diag, mask[:, :].rearrange("p (f h k) -> p f h k", f=1, h=1)
                                         .to_broadcast([P, 2, TH, P]), ALU.add))
                dve.tensor_reduce(nmax[:, own, 0:1], ps[:, b:b + 2, 0:P], AX.X, ALU.max, negate=True)
                dve.tensor_reduce(nmax[:, own, 1:2], ps[:, b:b + 2, P:P + S], AX.X, ALU.max,
                                  negate=True).then_inc(max_ready, 1)

            def normalise(g, pair):
                j = 2 * JOBS.index(g) + pair
                dve.wait_ge(exp_done, j + 1)
                own = slice(2 * pair, 2 * pair + 2)
                settle(dve.reciprocal(rsum[:, own, :], sums[:, own, :]))
                for h in range(TH):
                    c, w = (h * M, M) if g == MEM_JOB else (h * P, P + h * P)
                    part = (probs_end if g == MEM_JOB else probs)[:, own, c:c + w]
                    m = dve.tensor_tensor(part, part, rsum[:, own, h:h + 1].to_broadcast([P, 2, w]), ALU.mult)
                m.then_inc(probs_ready, 1)

            def pool_windows():
                dve.wait_ge(evacuated, U + 1)
                dve.wait_ge(pads_zero, 3)
                dve.wait_ge(consts_ready, 3 + NF)
                src = u_pad
                for i in range(NF):
                    dst, sh = (sum_a, sum_b)[i % 2], 1 << i
                    settle(dve.tensor_tensor(dst[:, i:, PAD:], src[:, i:, PAD:], src[:, i:, PAD - sh:PAD - sh + S],
                                             ALU.add))
                    src = dst
                for i, w in enumerate(WINDOWS):
                    total = (sum_a, sum_b)[i % 2]
                    first = slice(PAD, PAD + WINDOWS[-1])
                    rest = slice(PAD + WINDOWS[-1], PAD + S)
                    settle(dve.tensor_tensor(total[:, i, first], total[:, i, first], inv_cnt[:, i, :], ALU.mult))
                    settle(dve.tensor_tensor(u_pad[:, i, first], total[:, i, first], u_pad[:, i, first], ALU.subtract))
                    dve.scalar_tensor_tensor(out=u_pad[:, i, rest], in0=total[:, i, rest], scalar=1.0 / w,
                                             in1=u_pad[:, i, rest], op0=ALU.mult, op1=ALU.subtract
                                             ).then_inc(pooled_ready, 1)

            dve.wait_ge(table_loaded, 1)
            dve.wait_ge(rows_turned, 1)
            dve.tensor_copy(mem_cols[:, :], ps[:, 0, 0:KT]).then_inc(cols_ready, 1)
            for b in range(2):
                turned_to_lo(memT, 0, b, 4)
                split_lo(b)
            split_lo(2)

            for n in range(PIECES):
                g, a = divmod(n, PPG)
                if a == PPG - 1 and g < OUT0:
                    dve.wait_ge(piece_used, n + 1)
                    evacuate(g)
                if g == MK and a + 2 < PPG:
                    turned_to_lo(memT, 0, a + 2, 4)
                if n == 0:
                    split_lo(3)
                for m in pieces_to_split(n):
                    split_lo(m)
                if g == MK and a == 5:
                    mean_square(0)
                if g == MK and a == 6:
                    dve.wait_ge(rstd_ready, 1)
                    for h in range(TH):
                        m = dve.tensor_scalar(diag[:, h], ident[:, :], rstd_in[:, 0, h:h + 1], None, ALU.mult)
                    m.then_inc(diag_ready, 1)
                if g == MV and a == 1:
                    mean_square(1)
                    dve.wait_ge(spread, 1)
                    dve.tensor_copy(x_cols[:, :], ps[:, 7, M:M + KT + NF]).then_inc(cols_ready, 1)
                    dve.tensor_copy(mem_rstd[:, 0, :], ps[:, 7, 0:M]).then_inc(spread_read, 1)
                if g == MV and a in (1, 2):
                    dve.wait_ge(rstd_ready, 2)
                    c = slice((a - 1) * D // 2, a * D // 2)
                    for h in range(TH):
                        m = dve.tensor_scalar(x_nat[:, h, c], x_nat[:, h, c], rstd_in[:, 1, h:h + 1], None, ALU.mult)
                    m.then_inc(scaled, 1)
                if g == MV and a in (3, 5):
                    for b in range(2 * (a - 3), 2 * (a - 3) + 4):
                        turned_to_lo(xT, 1, b, 0)
                if g in JOBS:
                    if a == 0:
                        mask_and_max(g, 0)
                        mask_and_max(g, 1)
                    if a == 1:
                        normalise(g, 0)
                    if a == 2:
                        normalise(g, 1)
                if g == GP and a == 0:
                    pool_windows()
                if g - 1 in GATES:
                    i = GATES.index(g - 1)
                    if a == 1:
                        dve.wait_ge(gate_att, i + 1)
                        dve.scalar_tensor_tensor(out=gate[:, :, :], in0=part_b[:, :, :], scalar=1.0, in1=gate[:, :, :],
                                                 op0=ALU.add, op1=ALU.mult).then_inc(y_ready, 1)
                    if a == 2:
                        dve.wait_ge(y_hi, i + 1)
                        own = slice(NF * i, NF * (i + 1))
                        dve.tensor_tensor(yT[:, own, 1], gate[:, :, :], yT[:, own, 0].bitcast(F32),
                                          ALU.subtract).then_inc(y_lo, 1)
                if OUT0 <= g < LAST and a == PPG - 1:
                    dve.wait_ge(piece_used, n + 1)
                    if g == OUT0:
                        dve.wait_ge(res_landed, 16 * TH)
                    c = (g - OUT0) * COLS
                    dve.tensor_tensor(x_res[:, :, c:c + COLS], ps[:, bank0(g):bank0(g) + TH, :],
                                      x_res[:, :, c:c + COLS], ALU.add).then_inc(summed, 1)
            dve.wait_ge(sq_done, TH * (LAST - OUT0))
            settle(dve.tensor_reduce(sst[:, :], ssq[:, :, 0:LAST - OUT0], AX.X, ALU.add))
            settle(dve.tensor_scalar(sst[:, :], sst[:, :], EPS, None, ALU.add))
            for h in range(TH):
                dve.wait_ge(half_used, h + 1)
                dve.tensor_tensor(x_res[:, h, end], ps[:, bank0(LAST) + h, :], x_res[:, h, end], ALU.add).then_inc(summed, 1)
                dve.wait_ge(summed, LAST - OUT0 + h + 1)
                dve.wait_ge(fg_landed, 16)
                dve.tensor_tensor(end_scaled[:, h], x_res[:, h, end], fg[:, end], ALU.mult).then_inc(end_weighted, 1)
                dve.wait_ge(sq_done, TH * (LAST - OUT0) + h + 1)
                dve.tensor_tensor(ms[:, h:h + 1], sst[:, h:h + 1], ssq[:, h, LAST - OUT0:], ALU.add).then_inc(ms2_ready, 1)
                dve.wait_ge(rstd2_ready, h + 1)
                dve.wait_ge(weighted, TH * (LAST - OUT0))
                for c in range(0, D - COLS, COLS):
                    dve.tensor_scalar(x_res[:, h, c:c + COLS], x_res[:, h, c:c + COLS], rstd[:, h:h + 1], None,
                                      ALU.mult).then_inc(finished_dve, 1)


_INS = ["x", "mem", "norm_g", "mem_norm_g", "w_in", "w_mem_kv", "w_pool", "pool_scale", "w_out", "final_norm_g"]


def kernel(**inputs):
    import numpy as _np
    import concourse.bacc as _bacc
    from concourse import mybir as _mybir
    from concourse.bass_utils import run_bass_kernel_spmd as _run

    nc = _bacc.Bacc("TRN2", target_bir_lowering=False, num_devices=1)
    arrays, args = {}, []
    for name in _INS:
        a = _np.ascontiguousarray(inputs[name])
        arrays[f"in_{name}"] = a
        args.append(nc.dram_tensor(f"in_{name}", a.shape, _mybir.dt.from_np(a.dtype), kind="ExternalInput").ap())
    args.append(nc.dram_tensor("out_0", (1, S, D), F32, kind="ExternalOutput").ap())
    build(nc, *args)
    r = _run(nc, [arrays], core_ids=[0])
    return r.results[0]["out_0"]
```
